# Optimizing a Trainium2 kernel written in Bass

```python
import jax, jax.numpy as jnp
from jax import lax
import numpy as np

D_MODEL = 1024
BATCH = 1
SEQ = 1024
DEPTH = 1

MIX_WIDTH = D_MODEL
POOL_WIDTH = MIX_WIDTH // 2
SGU_WIDTH = MIX_WIDTH - POOL_WIDTH
POOL_WINDOWS = (2, 4, 8, 16)
POOL_GROUPS = len(POOL_WINDOWS)
POOL_GROUP_DIM = POOL_WIDTH // POOL_GROUPS
SGU_CHUNK = 128
SGU_HEADS = 4
SGU_HEAD_DIM = SGU_WIDTH // SGU_HEADS
IN_PROJ_WIDTH = POOL_WIDTH + 2 * SGU_WIDTH
PEER_HEADS = 8
PEER_N_KEYS = 128
PEER_N_EXPERTS = PEER_N_KEYS * PEER_N_KEYS
PEER_D_KEY = 256
PEER_HALF = PEER_D_KEY // 2
PEER_TOPK = 16
PEER_TOKEN_BLOCK = 128
N_MOD = 6
EPS = 1e-6

kernel_name = "hybrid_pool_sgu_peer_adaln"

def rms_norm(x, g):
    xf = x.astype(jnp.float32)
    y = xf * lax.rsqrt(jnp.mean(xf * xf, axis=-1, keepdims=True) + EPS)
    return (y * g.astype(jnp.float32)).astype(x.dtype)

def layer_norm(x, g, b):
    xf = x.astype(jnp.float32)
    mu = jnp.mean(xf, axis=-1, keepdims=True)
    xc = xf - mu
    y = xc * lax.rsqrt(jnp.mean(xc * xc, axis=-1, keepdims=True) + EPS)
    return (y * g.astype(jnp.float32) + b.astype(jnp.float32)).astype(x.dtype)

def modulate(h, shift, scale):
    return h * (1 + scale) + shift

def pool_mixer(a, w_pool, pool_scale):
    B, S, _ = a.shape
    af = a.astype(jnp.float32).reshape(B, S, POOL_GROUPS, POOL_GROUP_DIM)
    cs = jnp.cumsum(af, axis=1)
    pos = jnp.arange(1, S + 1, dtype=jnp.float32)
    outs = []
    for g, w in enumerate(POOL_WINDOWS):
        c_g = cs[:, :, g]
        prev = jnp.pad(c_g, ((0, 0), (w, 0), (0, 0)))[:, :S]
        mean = (c_g - prev) / jnp.minimum(pos, float(w))[None, :, None]
        outs.append(mean - af[:, :, g])
    pooled = jnp.stack(outs, axis=2)
    y = jnp.einsum('bsgc,gcd->bsgd', pooled, w_pool.astype(jnp.float32))
    y = y.reshape(B, S, POOL_WIDTH) * pool_scale.astype(jnp.float32)
    return y.astype(a.dtype)

def spatial_gating(u, v, ln_g, ln_b, w_spatial, b_spatial):
    B, S, _ = u.shape
    n = S // SGU_CHUNK
    vn = layer_norm(v, ln_g, ln_b).astype(jnp.float32)
    vn = vn.reshape(B, n, SGU_CHUNK, SGU_HEADS, SGU_HEAD_DIM)
    mask = jnp.tril(jnp.ones((SGU_CHUNK, SGU_CHUNK), dtype=bool))
    w = jnp.where(mask[None], w_spatial.astype(jnp.float32), 0.0)
    mixed = jnp.einsum('hts,bnshc->bnthc', w, vn)
    mixed = mixed + b_spatial.astype(jnp.float32).T[None, None, :, :, None]
    uf = u.astype(jnp.float32).reshape(B, n, SGU_CHUNK, SGU_HEADS, SGU_HEAD_DIM)
    return (uf * mixed).reshape(B, S, SGU_WIDTH).astype(u.dtype)

def peer_ffn(h, w_query, sub_keys, expert_down, expert_up):
    B, S, D = h.shape
    tokens = h.reshape(-1, PEER_TOKEN_BLOCK, D)

    def block(xb):
        T = xb.shape[0]
        q = (xb @ w_query).astype(jnp.float32).reshape(T, PEER_HEADS, 2, PEER_HALF)
        scores = jnp.einsum('thpd,hpkd->thpk', q, sub_keys.astype(jnp.float32))
        s_top, i_top = lax.top_k(scores, PEER_TOPK)
        cand = s_top[:, :, 0, :, None] + s_top[:, :, 1, None, :]
        cand_idx = i_top[:, :, 0, :, None] * PEER_N_KEYS + i_top[:, :, 1, None, :]
        cand = cand.reshape(T, PEER_HEADS, PEER_TOPK * PEER_TOPK)
        cand_idx = cand_idx.reshape(T, PEER_HEADS, PEER_TOPK * PEER_TOPK)
        best, sel = lax.top_k(cand, PEER_TOPK)
        idx = jnp.take_along_axis(cand_idx, sel, axis=-1)
        gate = jax.nn.softmax(best, axis=-1)
        u_e = expert_down[idx]
        v_e = expert_up[idx]
        act = jax.nn.gelu(jnp.einsum('thkd,td->thk', u_e, xb).astype(jnp.float32), approximate=False)
        return jnp.einsum('thk,thkd->td', (gate * act).astype(xb.dtype), v_e)

    return lax.map(block, tokens).reshape(B, S, D)

def setup_inputs(seed: int = 0) -> dict:
    key = jax.random.key(seed)
    ks = jax.random.split(key, 20)
    f = jnp.float32
    D = D_MODEL
    L = DEPTH
    nrm = lambda k, shape, s: jax.random.normal(k, shape, f) * s
    return {
        "x": nrm(ks[0], (BATCH, SEQ, D), 1.0),
        "c": nrm(ks[1], (BATCH, D), 1.0),
        "w_ada": nrm(ks[2], (L, D, N_MOD * D), 0.5 * D ** -0.5),
        "b_ada": nrm(ks[3], (L, N_MOD * D), 0.02),
        "g_norm1": 1.0 + nrm(ks[4], (L, D), 0.05),
        "w_in": nrm(ks[5], (L, D, IN_PROJ_WIDTH), D ** -0.5),
        "w_pool": nrm(ks[6], (L, POOL_GROUPS, POOL_GROUP_DIM, POOL_GROUP_DIM), POOL_GROUP_DIM ** -0.5),
        "pool_scale": 1.0 + nrm(ks[7], (L, POOL_WIDTH), 0.1),
        "sgu_ln_g": 1.0 + nrm(ks[8], (L, SGU_WIDTH), 0.05),
        "sgu_ln_b": nrm(ks[9], (L, SGU_WIDTH), 0.02),
        "w_spatial": nrm(ks[10], (L, SGU_HEADS, SGU_CHUNK, SGU_CHUNK), SGU_CHUNK ** -0.5),
        "b_spatial": 1.0 + nrm(ks[11], (L, SGU_HEADS, SGU_CHUNK), 0.05),
        "w_out": nrm(ks[12], (L, MIX_WIDTH, D), MIX_WIDTH ** -0.5),
        "g_norm2": 1.0 + nrm(ks[13], (L, D), 0.05),
        "w_query": nrm(ks[14], (L, D, PEER_HEADS * PEER_D_KEY), D ** -0.5),
        "sub_keys": nrm(ks[15], (L, PEER_HEADS, 2, PEER_N_KEYS, PEER_HALF), PEER_HALF ** -0.5),
        "expert_down": nrm(ks[16], (L, PEER_N_EXPERTS, D), D ** -0.5),
        "expert_up": nrm(ks[17], (L, PEER_N_EXPERTS, D), PEER_HEADS ** -0.5),
        "g_final": 1.0 + nrm(ks[18], (D,), 0.05),
    }

def reference(x, c, w_ada, b_ada, g_norm1, w_in, w_pool, pool_scale, sgu_ln_g, sgu_ln_b, w_spatial, b_spatial, w_out, g_norm2, w_query, sub_keys, expert_down, expert_up, g_final):
    c_act = jax.nn.silu(c)
    for l in range(DEPTH):
        mod = jnp.einsum('bd,de->be', c_act, w_ada[l]) + b_ada[l]
        shift1, scale1, gate1, shift2, scale2, gate2 = jnp.split(mod[:, None, :], N_MOD, axis=-1)
        h = modulate(rms_norm(x, g_norm1[l]), shift1, scale1)
        proj = h @ w_in[l]
        a = proj[..., :POOL_WIDTH]
        u = proj[..., POOL_WIDTH:POOL_WIDTH + SGU_WIDTH]
        v = proj[..., POOL_WIDTH + SGU_WIDTH:]
        mixed = jnp.concatenate([
            pool_mixer(a, w_pool[l], pool_scale[l]),
            spatial_gating(u, v, sgu_ln_g[l], sgu_ln_b[l], w_spatial[l], b_spatial[l]),
        ], axis=-1)
        x = x + gate1 * (mixed @ w_out[l])
        h = modulate(rms_norm(x, g_norm2[l]), shift2, scale2)
        x = x + gate2 * peer_ffn(h, w_query[l], sub_keys[l], expert_down[l], expert_up[l])
    return rms_norm(x, g_final)


_drawn_inputs = setup_inputs


def setup_inputs(seed=0):
    import zlib

    import numpy as np

    out = dict(_drawn_inputs(seed))
    spreads = {}
    factors = {'g_norm1': 2.98,
     'pool_scale': 2.839,
     'sgu_ln_g': 6.421,
     'sgu_ln_b': 27.971,
     'b_spatial': 4.462,
     'g_norm2': 14.271}
    for name, (base, spread) in spreads.items():
        noise = np.random.default_rng([zlib.crc32(name.encode()), seed]).standard_normal(out[name].shape)
        drawn = base * np.exp(spread * noise) if base else spread * noise
        out[name] = __import__('jax').numpy.asarray(drawn.astype(out[name].dtype))
    for name, factor in factors.items():
        out[name] = (out[name] * factor).astype(out[name].dtype)
    return out
```

```python
from contextlib import ExitStack

import numpy as np
import concourse.bass as bass
from concourse import mybir

F32 = mybir.dt.float32
U32 = mybir.dt.uint32
BF16 = mybir.dt.bfloat16
ALU = mybir.AluOpType
ACT = mybir.ActivationFunctionType
AX_X = mybir.AxisListType.X

P = 128
D = 1024
SEQ = 1024
TILES = SEQ // P
KC = D // P
HALF = 512
POOL_WINDOWS = (2, 4, 8, 16)
GROUPS = len(POOL_WINDOWS)
IN_WIDTH = 3 * HALF
N_MOD = 6
HEADS = 8
SIDES = 2 * HEADS
KEYS = 128
TOPK = 16
SLOTS = HEADS * TOPK
EPS = 1e-6
LOWEST = -3.0e38

PAIR = 2
PAIRS = HEADS // PAIR
RING = 8
TURN = PAIR * TOPK
ROUTE_STEPS = 15
OPEN = 1

C_IDENT = 0
C_FIRST = P
C_BAND = C_FIRST + GROUPS * P
C_PREV = C_BAND + GROUPS * P
C_TRIL = C_PREV + GROUPS * P
C_IOTA = C_TRIL + P
C_EPS = C_IOTA + TOPK
C_ALL = C_EPS + 1


def shape_constants():
    out = np.zeros((P, C_ALL), np.float32)
    out[:, C_IDENT:C_IDENT + P] = np.eye(P)
    s, t = np.arange(P)[:, None], np.arange(P)[None, :]
    for g, w in enumerate(POOL_WINDOWS):
        near = (s <= t) & (s > t - w)
        eye = (s == t).astype(np.float32)
        out[:, C_FIRST + g * P:C_FIRST + (g + 1) * P] = near / np.minimum(t + 1.0, w) - eye
        out[:, C_BAND + g * P:C_BAND + (g + 1) * P] = near / float(w) - eye
        out[:, C_PREV + g * P:C_PREV + (g + 1) * P] = (s - P > t - w) / float(w)
    out[:, C_TRIL:C_TRIL + P] = s <= t
    out[:, C_IOTA:C_EPS] = np.arange(TOPK)
    out[:, C_EPS] = EPS
    return out


def build(nc, x, c, w_ada, b_ada, g_norm1, w_in, w_pool, pool_scale, sgu_ln_g, sgu_ln_b, w_spatial_t,
          b_spatial, w_out, g_norm2, w_query_t, sub_keys_t, experts, g_final, constants, x1_dram, out):
    with ExitStack() as ctx:
        def sb(name, shape, dt=F32):
            return ctx.enter_context(nc.sbuf_tensor(name, shape, dt))

        def sem(name):
            return ctx.enter_context(nc.semaphore(name))

        region_a = sb("region_a", [P, 20 * 1024])
        w_in_sb = region_a[:, 0:KC * IN_WIDTH].rearrange("p (k n) -> p k n", k=KC)
        w_out_sb = region_a[:, KC * IN_WIDTH:KC * (IN_WIDTH + D)].rearrange("p (k n) -> p k n", k=KC)
        wq_t = region_a[:, 0:SIDES * D].rearrange("p (s d) -> p s d", s=SIDES)
        keys_t = region_a[:, SIDES * D:SIDES * D + SIDES * KEYS].rearrange("p (s k) -> p s k", s=SIDES)
        ring = region_a[:, 0:RING * 2 * D].rearrange("p (r n) -> p r n", r=RING)
        SPARE = RING * 2 * D
        h2_cur = region_a[:, SPARE:SPARE + D]
        squares = region_a[:, SPARE + D:SPARE + 2 * D]
        x1_fin = region_a[:, SPARE + 2 * D:SPARE + 3 * D]
        y = region_a[:, SPARE + 3 * D:SPARE + 4 * D]

        region_b = sb("region_b", [P, 16 * 1024])
        key_map = region_b[:, :].rearrange("p (k n) -> p k n", k=KC)
        ADA_W = KC * HALF
        ada_stage = [region_b[:, (2 + i) * ADA_W:(3 + i) * ADA_W].rearrange("p (k n) -> p k n", k=KC)
                     for i in range(2)]
        at = [0]

        def temp(n):
            at[0] += n
            assert at[0] <= 2 * ADA_W
            return region_b[:, at[0] - n:at[0]]

        x_in = temp(D)
        x_res = temp(D)
        h = temp(D)
        h_t = temp(D).rearrange("p (k t) -> p k t", k=KC)
        mixed_t = temp(D).rearrange("p (k t) -> p k t", k=KC)
        vn = temp(HALF)
        u_t = temp(HALF)
        pooled_t = temp(HALF)
        gated = temp(HALF)
        a_prev = temp(HALF)
        a_cur = temp(HALF)

        mod = sb("mod", [P, N_MOD, D])
        SHIFT1, SCALE1, GATE1, SHIFT2, SCALE2, GATE2 = range(N_MOD)
        gf = sb("gf", [P, D])
        const = sb("const", [P, C_ALL])
        ident = const[:, C_IDENT:C_IDENT + P]
        band_cur = const[:, C_FIRST:C_FIRST + GROUPS * P]
        band_gen = const[:, C_BAND:C_BAND + GROUPS * P]
        band_prev = const[:, C_PREV:C_PREV + GROUPS * P]
        tril_t = const[:, C_TRIL:C_TRIL + P]
        iota16 = const[:, C_IOTA:C_IOTA + TOPK]
        eps = const[:, C_EPS:C_EPS + 1]
        small_w = sb("small_w", [P, 4 * HALF])
        w_pool_sb = small_w[:, 0:HALF]
        w_sp_t = small_w[:, HALF:2 * HALF]
        b_sp = small_w[:, 2 * HALF:3 * HALF]
        ln_g = small_w[:, 3 * HALF:4 * HALF]
        ln_b = sb("ln_b", [P, HALF])
        p_scale = sb("p_scale", [P, GROUPS])
        c_cols = sb("c_cols", [P, KC])
        c_act = sb("c_act", [P, KC])

        x1_next = sb("x1_next", [P, D])
        h2_next = sb("h2_next", [P, D])
        h2_t = sb("h2_t", [P, KC, P])
        c_wide = h2_t
        g1, g2 = x1_next, h2_next
        diag = sb("diag", [P, RING, P])
        x1 = diag[:, :, :].rearrange("p r t -> p (r t)")

        score = small_w[:, 0:HALF].rearrange("p (b k) -> p b k", b=4)
        cand = small_w[:, HALF:2 * HALF].rearrange("p (h k) -> p h k", h=PAIR)
        cand2 = small_w[:, 2 * HALF:3 * HALF].rearrange("p (h k) -> p h k", h=PAIR)
        score2 = small_w[:, 2 * HALF:3 * HALF].rearrange("p (b k) -> p b k", b=4)
        logits, expd, gate = (small_w[:, 3 * HALF + i * SLOTS:3 * HALF + (i + 1) * SLOTS] for i in range(3))
        act_in, act_out, weight = (small_w[:, 3 * HALF + 3 * SLOTS + i * TURN:3 * HALF + 3 * SLOTS + (i + 1) * TURN]
                                   for i in range(3))
        top_s, top_f = (band_cur[:, i * 4 * TOPK:(i + 1) * 4 * TOPK].rearrange("p (b k) -> p b k", b=4)
                        for i in range(2))
        sel_f, found = (band_gen[:, i * 2 * TURN:(i + 1) * 2 * TURN].rearrange("p (e h k) -> p e h k", e=2, h=PAIR)
                        for i in range(2))
        best = band_prev[:, 0:TURN].rearrange("p (h k) -> p h k", h=PAIR)
        top_i = sb("top_i", [P, 4, TOPK], U32)
        sel = sb("sel", [P, PAIR, TOPK], U32)
        sel_ab = sb("sel_ab", [P, 2, PAIR, TOPK], U32)
        expert_rows = sb("expert_rows", [P, SLOTS], U32)
        row_stage = [sb(f"row_stage{i}", [P, TOPK], U32) for i in range(PAIR)]
        stat = sb("stat", [P, 16])
        v_stats = sb("v_stats", [P, 6])
        v_mean_var = sb("v_mean_var", [P, 2])
        sums = sb("sums", [P, 2, HEADS])
        zero_bf = ln_b[:, 0:HALF // 2].bitcast(BF16)

        banks = [ctx.enter_context(nc.psum_tensor(f"banks{i}", [P, D], F32)) for i in range(4)]
        ps_wide = banks[0]
        ps_v, ps_a = banks[1][:, 0:HALF], banks[1][:, HALF:D]
        ps_u, ps_pool = banks[2][:, 0:HALF], banks[2][:, HALF:D]
        ps_y, ps_sgu = banks[3][:, 0:HALF], banks[3][:, HALF:D]
        ps_ada = [banks[3][:, 0:HALF], banks[3][:, HALF:D]]
        ps_fold = [banks[1], banks[2]]
        ps_h2 = banks[1]
        ps_score = banks[2][:, 0:HALF]
        ps_sum = banks[0]

        s_const = sem("const_loaded")
        s_rows = sem("row_vectors_loaded")
        s_small = sem("small_weights_loaded")
        s_ada_w = [sem("ada_stage0_loaded"), sem("ada_stage1_loaded")]
        s_w_in = sem("w_in_loaded")
        s_w_out = sem("w_out_loaded")
        s_x_in = sem("x_in_loaded")
        s_x_res = sem("x_res_loaded")
        s_cact = sem("c_act_ready")
        s_cwide = sem("c_wide_ready")
        s_ada_ps = sem("ada_psum_ready")
        s_mod = sem("mod_rows_ready")
        s_scales = sem("scales_folded")
        s_masked = sem("w_spatial_masked")
        s_init = sem("start_values_set")
        s_ssq1 = sem("ssq1_ready")
        s_norm1 = sem("norm1_steps")
        s_h = sem("h_ready")
        s_tr = sem("h_transposed")
        s_ht = sem("h_t_ready")
        s_v = sem("v_psum_ready")
        s_a = sem("a_psum_ready")
        s_u = sem("u_psum_ready")
        s_ln = sem("ln_steps")
        s_v_root = sem("v_root_ready")
        s_a_sb = sem("a_ready")
        s_u_sb = sem("u_t_ready")
        s_pool = sem("pool_psum_ready")
        s_turned = sem("pool_state_turned")
        s_pooled = sem("pooled_ready")
        s_y = sem("y_psum_ready")
        s_sgu = sem("sgu_psum_ready")
        s_gated = sem("gated_ready")
        s_mixed = sem("mixed_ready")
        s_o = sem("out_psum_ready")
        s_x1 = sem("x1_steps")
        s_x1_st = sem("x1_stored")
        s_x1_free = sem("x1_free")
        s_wq = [sem(f"w_query{n}_loaded") for n in range(4)]
        s_keys = sem("keys_loaded")
        s_fold = sem("fold_psum_ready")
        s_fold_a = sem("key_map_by_act")
        s_fold_v = sem("key_map_by_vector")
        s_x1n = sem("x1_next_loaded")
        s_ssq2 = sem("ssq2_ready")
        s_norm2 = sem("norm2_steps")
        s_h2 = sem("h2_ready")
        s_tr2 = sem("h2_transposed")
        s_h2t = sem("h2_t_ready")
        s_score = sem("score_psum_ready")
        s_score_sb = sem("score_ready")
        s_route = sem("route_steps")
        s_staged = sem("rows_staged")
        s_exp = sem("exp_ready")
        s_soft = sem("softmax_steps")
        s_h2c = sem("h2_cur_ready")
        s_row = [sem(f"expert_row{r}_landed") for r in range(RING)]
        s_free = sem("ring_slots_free")
        s_dots = sem("dots_ready")
        s_gelu = sem("gelu_ready")
        s_weight = sem("weights_ready")
        s_diag = sem("diags_ready")
        s_zeroed = sem("sums_zeroed")
        s_sum = sem("sums_ready")
        s_fin = sem("final_steps")
        s_ssq3 = sem("ssq3_ready")
        s_rms = sem("final_norm_steps")
        s_x1f = sem("x1_final_loaded")
        s_out = sem("out_stored")
        s_y_free = sem("y_free")

        x_v = x.rearrange("b (t p) d -> (b t) p d", p=P)
        out_v = out.rearrange("b (t p) d -> (b t) p d", p=P)
        ada_v = w_ada.rearrange("l (p k) n -> (l p) k n", k=KC)
        w_in_v = w_in.rearrange("l (k p) n -> p (l k) n", p=P)
        w_out_v = w_out.rearrange("l (k p) n -> p (l k) n", p=P)

        block = ctx.enter_context(nc.Block())

        def spread(row, n):
            return row.rearrange("a n -> (a n)")[0:n].partition_broadcast(P)

        def apart(engine):
            engine.nop(nofuse=True)

        @block.sync
        def _(sp):
            sp.sem_inc(s_x1_free, OPEN)
            sp.sem_inc(s_y_free, OPEN)
            sp.dma_start(c_cols[:, :], c.rearrange("b (p k) -> (b p) k", k=KC)).then_inc(s_const, 16)
            sp.dma_start(const[:, :], constants).then_inc(s_const, 16)

            def load_ada(j):
                if j >= 2:
                    sp.wait_ge(s_ada_ps, j - 1)
                sp.dma_start(ada_stage[j % 2], ada_v[:, :, j * HALF:(j + 1) * HALF]).then_inc(s_ada_w[j % 2], 16)

            load_ada(0)
            load_ada(1)
            sp.dma_start(mod[:, :, :].rearrange("p m d -> p (m d)"), b_ada.partition_broadcast(P)).then_inc(s_rows, 16)
            sp.dma_start(g1[:, :], g_norm1.partition_broadcast(P)).then_inc(s_rows, 16)
            sp.dma_start(g2[:, :], g_norm2.partition_broadcast(P)).then_inc(s_rows, 16)
            sp.dma_start(gf[:, :], g_final.partition_broadcast(P)).then_inc(s_rows, 16)
            load_ada(2)
            load_ada(3)
            sp.dma_start(x_in, x_v[0]).then_inc(s_x_in, 16)
            sp.dma_start(w_pool_sb.rearrange("p (g d) -> p g d", g=GROUPS),
                         w_pool.rearrange("l g c d -> c (l g) d")).then_inc(s_small, 16)
            sp.dma_start(w_sp_t, w_spatial_t).then_inc(s_small, 16)
            sp.dma_start(b_sp, b_spatial.partition_broadcast(P)).then_inc(s_small, 16)
            sp.dma_start(ln_g, sgu_ln_g.partition_broadcast(P)).then_inc(s_small, 16)
            sp.dma_start(ln_b[:, :], sgu_ln_b.partition_broadcast(P)).then_inc(s_small, 16)
            sp.dma_start(p_scale[:, :], pool_scale).then_inc(s_small, 16)
            for j in range(4, 2 * N_MOD):
                load_ada(j)
                if j == 5:
                    sp.dma_start(w_in_sb[:, 0:KC // 2, :], w_in_v[:, 0:KC // 2, :]).then_inc(s_w_in, 16)
                if j == 7:
                    sp.dma_start(w_in_sb[:, KC // 2:KC, :], w_in_v[:, KC // 2:KC, :]).then_inc(s_w_in, 16)
                if j == 9:
                    sp.dma_start(w_out_sb, w_out_v).then_inc(s_w_out, 16)

            def mixer_loads(t):
                sp.wait_ge(s_norm1, 2 * t)
                sp.dma_start(x_in, x_v[t]).then_inc(s_x_in, 16)
                if not isinstance(t, int) or t >= 2:
                    sp.wait_ge(s_x1, OPEN + 2 * (t - 1))
                sp.dma_start(x_res, x_v[t - 1]).then_inc(s_x_res, 16)

            def store_x1(t):
                sp.wait_ge(s_x1, OPEN + 2 * (t + 1))
                sp.dma_start(x1_dram[t], x1).then_inc(s_x1_st, 16)
                sp.wait_ge(s_x1_st, 16 * (t + 1))
                sp.sem_inc(s_x1_free, 1)

            mixer_loads(1)
            with sp.Fori(2, TILES) as t:
                mixer_loads(t)
                store_x1(t - 2)
            sp.wait_ge(s_x1, OPEN + 2 * (TILES - 1))
            sp.dma_start(x_res, x_v[TILES - 1]).then_inc(s_x_res, 16)
            store_x1(TILES - 2)

            sp.wait_ge(s_u, TILES)
            in_w_in = KC * IN_WIDTH // D
            wq_v = w_query_t
            for n in range(3):
                a, b = n * in_w_in // 3, (n + 1) * in_w_in // 3
                sp.dma_start(wq_t[:, a:b, :], wq_v[:, a:b, :]).then_inc(s_wq[n], 16)
            sp.wait_ge(s_o, OPEN + TILES)
            sp.dma_start(keys_t, sub_keys_t).then_inc(s_keys, 16)
            sp.dma_start(wq_t[:, in_w_in:SIDES, :], wq_v[:, in_w_in:SIDES, :]).then_inc(s_wq[3], 16)
            store_x1(TILES - 1)

            sp.wait_ge(s_scales, 2)
            sp.dma_start(x1_next[:, :], x1_dram[0]).then_inc(s_x1n, 16)

            def expert_loads(t, last):
                sp.wait_ge(s_fin, OPEN + 4 * t)
                sp.dma_start(x1_fin, x1_dram[t]).then_inc(s_x1f, 16)
                if not last:
                    sp.wait_ge(s_norm2, 2 * (t + 2))
                    sp.dma_start(x1_next[:, :], x1_dram[t + 2]).then_inc(s_x1n, 16)
                sp.wait_ge(s_fin, OPEN + 4 * (t + 1))
                sp.dma_start(out_v[t], y).then_inc(s_out, 16)
                sp.wait_ge(s_out, 16 * (t + 1))
                sp.sem_inc(s_y_free, 1)

            sp.wait_ge(s_norm2, 2)
            sp.dma_start(x1_next[:, :], x1_dram[1]).then_inc(s_x1n, 16)
            sp.wait_ge(s_h2c, 1)
            with sp.Fori(0, TILES - 2) as t:
                expert_loads(t, False)
            expert_loads(TILES - 2, True)
            expert_loads(TILES - 1, True)

        @block.gpsimd
        def _(pool):
            pool.sem_inc(s_turned, OPEN)
            nc.gpsimd.memset(a_prev, 0.0).then_inc(s_init, 1)

            def turn_pool_state(t):
                pool.wait_ge(s_pool, t + 1)
                apart(pool)
                nc.gpsimd.tensor_copy(a_prev, a_cur)
                nc.gpsimd.tensor_copy(band_cur, band_gen).then_inc(s_turned, 1)

            with pool.Fori(0, TILES - 1) as t:
                turn_pool_state(t)

            def gather_turn(t, q):
                turn = t * PAIRS + q
                for i in range(PAIR):
                    pool.wait_ge(s_route, OPEN + ROUTE_STEPS * (turn + 1))
                    pool.wait_ge(s_free, turn * TURN + i * TOPK + 1)
                    apart(pool)
                    nc.gpsimd.tensor_copy(row_stage[i][:, :],
                                          expert_rows[:, bass.ds((q * PAIR + i) * TOPK, TOPK)]).then_inc(s_staged, 1)
                    pool.wait_ge(s_staged, turn * PAIR + i + 1)
                    for k in range(TOPK):
                        s = i * TOPK + k
                        pool.wait_ge(s_free, turn * TURN + s + 1)
                        apart(pool)
                        nc.gpsimd.indirect_dma_start(
                            ring[:, s % RING, :], None, experts,
                            bass.IndirectOffsetOnAxis(ap=row_stage[i][:, k:k + 1], axis=0),
                        ).then_inc(s_row[s % RING], 16)

            pool.wait_ge(s_fold, SIDES)
            with pool.Fori(0, TILES) as t:
                with pool.Fori(0, PAIRS) as q:
                    gather_turn(t, q)

        @block.tensor
        def _(pe):
            pe.sem_inc(s_y, OPEN)
            pe.sem_inc(s_o, OPEN)
            pe.wait_ge(s_cwide, 1)
            for j in range(2 * N_MOD):
                pe.wait_ge(s_ada_w[j % 2], 16 * (j // 2 + 1))
                if j >= 2:
                    pe.wait_ge(s_mod, j - 1)
                for k in range(KC):
                    last = nc.tensor.matmul(ps_ada[j % 2], c_wide[:, k, :], ada_stage[j % 2][:, k, :],
                                            start=(k == 0), stop=(k == KC - 1))
                last.then_inc(s_ada_ps, 1)

            def transposes(t):
                pe.wait_ge(s_h, t + 1)
                for k in range(KC):
                    last = nc.tensor.transpose(ps_wide[:, k * P:(k + 1) * P], h[:, k * P:(k + 1) * P], ident)
                    if k % 4 == 3:
                        last.then_inc(s_tr, 1)

            def projection(t):
                pe.wait_ge(s_ht, 2 * (t + 1))
                for k in range(KC):
                    last = nc.tensor.matmul(ps_v, h_t[:, k, :], w_in_sb[:, k, 2 * HALF:3 * HALF],
                                            start=(k == 0), stop=(k == KC - 1))
                last.then_inc(s_v, 1)
                for k in range(KC):
                    last = nc.tensor.matmul(ps_a, h_t[:, k, :], w_in_sb[:, k, 0:HALF],
                                            start=(k == 0), stop=(k == KC - 1))
                last.then_inc(s_a, 1)
                for g in range(GROUPS):
                    for k in range(KC):
                        last = nc.tensor.matmul(ps_u[:, g * P:(g + 1) * P],
                                                w_in_sb[:, k, HALF + g * P:HALF + (g + 1) * P], h_t[:, k, :],
                                                start=(k == 0), stop=(k == KC - 1))
                last.then_inc(s_u, 1)

            def mix(t):
                pe.wait_ge(s_a_sb, t + 1)
                pe.wait_ge(s_turned, OPEN + t)
                for g in range(GROUPS):
                    cols = slice(g * P, (g + 1) * P)
                    nc.tensor.matmul(ps_pool[:, cols], a_cur[:, cols], band_cur[:, cols], start=True, stop=False)
                    last = nc.tensor.matmul(ps_pool[:, cols], a_prev[:, cols], band_prev[:, cols],
                                            start=False, stop=True)
                last.then_inc(s_pool, 1)
                pe.wait_ge(s_ln, 6 * (t + 1))
                for g in range(GROUPS):
                    cols = slice(g * P, (g + 1) * P)
                    last = nc.tensor.matmul(ps_sgu[:, cols], vn[:, cols], w_sp_t[:, cols], start=True, stop=True)
                last.then_inc(s_sgu, 1)
                pe.wait_ge(s_pooled, t + 1)
                for g in range(GROUPS):
                    cols = slice(g * P, (g + 1) * P)
                    last = nc.tensor.matmul(ps_y[:, cols], w_pool_sb[:, cols], pooled_t[:, cols], start=True, stop=True)
                last.then_inc(s_y, 1)
                pe.wait_ge(s_mixed, 2 * (t + 1))
                for n in range(2):
                    for i, k in enumerate([*range(GROUPS, KC), *range(GROUPS)]):
                        last = nc.tensor.matmul(ps_wide[:, n * HALF:(n + 1) * HALF], mixed_t[:, k, :],
                                                w_out_sb[:, k, n * HALF:(n + 1) * HALF],
                                                start=(i == 0), stop=(i == KC - 1))
                last.then_inc(s_o, 1)

            transposes(0)
            pe.wait_ge(s_w_in, 32)
            projection(0)
            pe.wait_ge(s_small, 96)
            pe.wait_ge(s_masked, 1)
            pe.wait_ge(s_init, 1)
            pe.wait_ge(s_w_out, 16)
            with pe.Fori(1, TILES) as t:
                pe.wait_ge(s_x1, OPEN + 2 * (t - 1))
                transposes(t)
                mix(t - 1)
                projection(t)
            mix(TILES - 1)

            pe.wait_ge(s_keys, 16)
            for s in range(SIDES):
                pe.wait_ge(s_wq[s // 4], 16)
                if s >= 2:
                    pe.wait_ge(s_fold_a, s - 1)
                    pe.wait_ge(s_fold_v, s - 1)
                for k in range(KC):
                    last = nc.tensor.matmul(ps_fold[s % 2][:, k * KEYS:(k + 1) * KEYS],
                                            wq_t[:, s, k * P:(k + 1) * P], keys_t[:, s, :], start=True, stop=True)
                last.then_inc(s_fold, 1)

            def transposes2(t):
                pe.wait_ge(s_h2, t + 1)
                for k in range(KC):
                    last = nc.tensor.transpose(ps_h2[:, k * P:(k + 1) * P], h2_next[:, k * P:(k + 1) * P], ident)
                    if k % 4 == 3:
                        last.then_inc(s_tr2, 1)

            def scores(t, q):
                pe.wait_ge(s_h2t, 2 * (t + 1))
                pe.wait_ge(s_score_sb, OPEN + t * PAIRS + q)
                for k in range(KC):
                    last = nc.tensor.matmul(ps_score, h2_t[:, k, :], key_map[:, k, bass.ds(q * 4 * KEYS, 4 * KEYS)],
                                            start=(k == 0), stop=(k == KC - 1))
                last.then_inc(s_score, 1)

            def clear_sums(stop):
                for n in range(2):
                    nc.tensor.matmul(ps_sum[:, n * HALF:(n + 1) * HALF], zero_bf[:, 0:P], zero_bf,
                                     start=not stop, stop=stop, skip_group_check=True)

            def add_expert(turn, s):
                pe.wait_ge(s_diag, turn * TURN + s + 1)
                for n in range(2):
                    last = nc.tensor.matmul(ps_sum[:, n * HALF:(n + 1) * HALF], diag[:, s % RING, :],
                                            ring[:, s % RING, D + n * HALF:D + (n + 1) * HALF],
                                            start=False, stop=False, skip_group_check=True)
                last.then_inc(s_free, 1)

            pe.wait_ge(s_fold_a, SIDES)
            pe.wait_ge(s_fold_v, SIDES)
            pe.wait_ge(s_zeroed, 1)
            pe.sem_inc(s_free, RING)

            def tile_turns(t, route, expert):
                if route:
                    transposes2(t)
                if expert:
                    pe.wait_ge(s_fin, OPEN + 4 * (t - 1))
                    clear_sums(False)
                with pe.Fori(0, PAIRS) as q:
                    if route:
                        scores(t, q)
                    if expert:
                        for s in range(TURN):
                            add_expert((t - 1) * PAIRS + q, s)
                if expert:
                    for n in range(2):
                        last = nc.tensor.matmul(ps_sum[:, n * HALF:(n + 1) * HALF], zero_bf[:, 0:P], zero_bf,
                                                start=False, stop=True, skip_group_check=True)
                    last.then_inc(s_sum, 1)

            tile_turns(0, True, False)
            with pe.Fori(1, TILES) as t:
                tile_turns(t, True, True)
            tile_turns(TILES, False, True)

        @block.scalar
        def _(act):
            act.sem_inc(s_score_sb, OPEN)
            act.wait_ge(s_const, 32)
            nc.scalar.activation(c_act[:, :], c_cols[:, :], ACT.Silu).then_inc(s_cact, 1)

            def root(mean_sq, out_col, steps, base, scale):
                act.wait_ge(steps, base + 1)
                nc.scalar.activation(out_col, mean_sq, ACT.Sqrt, bias=eps, scale=scale).then_inc(steps, 1)

            def square1(t):
                act.wait_ge(s_x_in, 16 * (t + 1))
                act.wait_ge(s_tr, 2 * t)
                nc.scalar.activation(h, x_in, ACT.Square, accum_out=stat[:, 0:1]).then_inc(s_ssq1, 1)
                root(stat[:, 0:1], stat[:, 1:2], s_ssq1, 2 * t, 1.0 / D)

            def copy_h_t(t):
                for n in range(2):
                    act.wait_ge(s_tr, 2 * t + n + 1)
                    act.wait_ge(s_u, t)
                    nc.scalar.copy(h_t[:, 4 * n:4 * n + 4, :].rearrange("p k t -> p (k t)"),
                                   ps_wide[:, n * HALF:(n + 1) * HALF]).then_inc(s_ht, 1)

            def copy_pooled(t):
                act.wait_ge(s_pool, t + 1)
                act.wait_ge(s_y, OPEN + t)
                nc.scalar.copy(pooled_t, ps_pool).then_inc(s_pooled, 1)

            def copy_a_u(t):
                act.wait_ge(s_ln, 6 * t + 2)
                nc.scalar.activation(stat[:, 12:13], v_mean_var[:, 1:2], ACT.Sqrt, bias=eps).then_inc(s_v_root, 1)
                act.wait_ge(s_a, t + 1)
                act.wait_ge(s_turned, OPEN + t)
                nc.scalar.copy(a_cur, ps_a).then_inc(s_a_sb, 1)
                act.wait_ge(s_u, t + 1)
                act.wait_ge(s_mixed, 2 * t)
                nc.scalar.copy(u_t, ps_u).then_inc(s_u_sb, 1)

            square1(0)
            copy_h_t(0)
            square1(1)
            copy_a_u(0)
            with act.Fori(1, TILES - 1) as t:
                copy_h_t(t)
                copy_pooled(t - 1)
                square1(t + 1)
                copy_a_u(t)
            copy_h_t(TILES - 1)
            copy_pooled(TILES - 2)
            copy_a_u(TILES - 1)
            copy_pooled(TILES - 1)

            act.wait_ge(s_o, OPEN + TILES)
            act.wait_ge(s_gated, TILES)
            act.wait_ge(s_x1, OPEN + 2 * TILES)
            act.wait_ge(s_mixed, 2 * TILES)
            for s in range(SIDES):
                act.wait_ge(s_fold, s + 1)
                nc.scalar.copy(key_map[:, 0:4, s * KEYS:(s + 1) * KEYS],
                               ps_fold[s % 2][:, 0:HALF].rearrange("p (k n) -> p k n", k=4)).then_inc(s_fold_a, 1)

            def square2(t):
                act.wait_ge(s_x1n, 16 * (t + 1))
                act.wait_ge(s_h2c, t)
                nc.scalar.activation(h2_next[:, :], x1_next[:, :], ACT.Square,
                                     accum_out=stat[:, 4:5]).then_inc(s_ssq2, 1)
                root(stat[:, 4:5], stat[:, 5:6], s_ssq2, 2 * t, 1.0 / D)

            def copy_h2_t(t):
                for n in range(2):
                    act.wait_ge(s_tr2, 2 * t + n + 1)
                    nc.scalar.copy(h2_t[:, 4 * n:4 * n + 4, :].rearrange("p k t -> p (k t)"),
                                   ps_h2[:, n * HALF:(n + 1) * HALF]).then_inc(s_h2t, 1)

            def copy_score(t, q):
                turn = t * PAIRS + q
                act.wait_ge(s_score, turn + 1)
                act.wait_ge(s_route, OPEN + ROUTE_STEPS * turn)
                nc.scalar.copy(score[:, :, :].rearrange("p b k -> p (b k)"), ps_score).then_inc(s_score_sb, 1)

            def expert_weight(turn, q, s):
                act.wait_ge(s_dots, turn * TURN + s + 1)
                nc.scalar.activation(act_out[:, s:s + 1], act_in[:, s:s + 1], ACT.Gelu).then_inc(s_gelu, 1)
                act.wait_ge(s_gelu, turn * TURN + s + 1)
                nc.scalar.mul(weight[:, s:s + 1], gate[:, bass.ds(q * TURN + s, 1)],
                              act_out[:, s:s + 1]).then_inc(s_weight, 1)
                act.wait_ge(s_weight, turn * TURN + s + 1)
                act.wait_ge(s_free, turn * TURN + s + 1)
                nc.scalar.mul(diag[:, s % RING, :], ident, weight[:, s:s + 1]).then_inc(s_diag, 1)

            def tile_turns(t, route, expert):
                if route:
                    square2(t)
                    copy_h2_t(t)
                with act.Fori(0, PAIRS) as q:
                    turn = (t - 1) * PAIRS + q
                    if expert:
                        act.wait_ge(s_soft, 3 * t)
                    if route and not expert:
                        copy_score(t, q)
                    if expert:
                        for s in range(TURN):
                            expert_weight(turn, q, s)
                            if route and s == 2:
                                copy_score(t, q)
                if route:
                    act.wait_ge(s_route, OPEN + ROUTE_STEPS * PAIRS * (t + 1))
                    nc.scalar.activation(expd[:, :], logits[:, :], ACT.Exp).then_inc(s_exp, 1)
                if expert:
                    act.wait_ge(s_fin, OPEN + 4 * (t - 1) + 2)
                    nc.scalar.activation(squares, y, ACT.Square, accum_out=stat[:, 8:9]).then_inc(s_ssq3, 1)
                    root(stat[:, 8:9], stat[:, 9:10], s_ssq3, 2 * (t - 1), 1.0 / D)

            tile_turns(0, True, False)
            with act.Fori(1, TILES) as t:
                tile_turns(t, True, True)
            tile_turns(TILES, False, True)

        @block.vector
        def _(dve):
            dve.sem_inc(s_x1, OPEN)
            dve.sem_inc(s_route, OPEN)
            dve.sem_inc(s_fin, OPEN)
            dve.wait_ge(s_cact, 1)
            nc.vector.tensor_copy(c_wide[:, :, :], c_act[:, :].unsqueeze(2).to_broadcast([P, KC, P])).then_inc(s_cwide, 1)
            dve.wait_ge(s_rows, 64)
            for j in range(2 * N_MOD):
                row = mod[:, j // 2, (j % 2) * HALF:(j % 2 + 1) * HALF]
                dve.wait_ge(s_ada_ps, j + 1)
                nc.vector.tensor_tensor(row, ps_ada[j % 2], row, ALU.add).then_inc(s_mod, 1)
                if j == 3:
                    dve.wait_ge(s_mod, 4)
                    nc.vector.scalar_tensor_tensor(out=mod[:, SCALE1, :], in0=mod[:, SCALE1, :], scalar=1.0,
                                                   in1=g1[:, :], op0=ALU.add, op1=ALU.mult).then_inc(s_scales, 1)
                if j == 9:
                    dve.wait_ge(s_mod, 10)
                    nc.vector.scalar_tensor_tensor(out=mod[:, SCALE2, :], in0=mod[:, SCALE2, :], scalar=1.0,
                                                   in1=g2[:, :], op0=ALU.add, op1=ALU.mult).then_inc(s_scales, 1)
            dve.wait_ge(s_small, 96)
            w_sp_v = w_sp_t.rearrange("p (g t) -> p g t", g=GROUPS)
            nc.vector.tensor_tensor(w_sp_v, w_sp_v, tril_t.unsqueeze(1).to_broadcast([P, GROUPS, P]),
                                    ALU.mult).then_inc(s_masked, 1)
            dve.wait_ge(s_scales, 2)

            def norm1(t):
                dve.wait_ge(s_ssq1, 2 * (t + 1))
                nc.vector.reciprocal(stat[:, 2:3], stat[:, 1:2]).then_inc(s_norm1, 1)
                dve.wait_ge(s_norm1, 2 * t + 1)
                nc.vector.scalar_tensor_tensor(out=h, in0=x_in, scalar=stat[:, 2:3], in1=mod[:, SCALE1, :],
                                               op0=ALU.mult, op1=ALU.mult).then_inc(s_norm1, 1)
                dve.wait_ge(s_norm1, 2 * t + 2)
                nc.vector.tensor_tensor(h, h, mod[:, SHIFT1, :], ALU.add).then_inc(s_h, 1)

            def layer_norm_v(t):
                dve.wait_ge(s_v, t + 1)
                nc.vector.bn_stats(v_stats[:, :], ps_v).then_inc(s_ln, 1)
                dve.wait_ge(s_ln, 6 * t + 1)
                apart(dve)
                nc.vector.bn_aggr(v_mean_var[:, :], v_stats[:, :]).then_inc(s_ln, 1)
                dve.wait_ge(s_v_root, t + 1)
                nc.vector.reciprocal(stat[:, 13:14], stat[:, 12:13]).then_inc(s_ln, 1)
                dve.wait_ge(s_ln, 6 * t + 3)
                dve.wait_ge(s_sgu, t)
                nc.vector.tensor_scalar(vn, ps_v, v_mean_var[:, 0:1], stat[:, 13:14],
                                        ALU.subtract, ALU.mult).then_inc(s_ln, 1)
                dve.wait_ge(s_ln, 6 * t + 4)
                nc.vector.tensor_tensor(vn, vn, ln_g, ALU.mult).then_inc(s_ln, 1)
                dve.wait_ge(s_ln, 6 * t + 5)
                nc.vector.tensor_tensor(vn, vn, ln_b[:, :], ALU.add).then_inc(s_ln, 1)

            def mix(t):
                dve.wait_ge(s_sgu, t + 1)
                nc.vector.tensor_tensor(gated, ps_sgu, b_sp, ALU.add).then_inc(s_gated, 1)
                dve.wait_ge(s_gated, t + 1)
                dve.wait_ge(s_u_sb, t + 1)
                dve.wait_ge(s_o, OPEN + t)
                nc.vector.tensor_tensor(mixed_t[:, GROUPS:KC, :].rearrange("p g t -> p (g t)"), gated, u_t,
                                        ALU.mult).then_inc(s_mixed, 1)
                dve.wait_ge(s_y, OPEN + t + 1)
                nc.vector.tensor_tensor(mixed_t[:, 0:GROUPS, :], ps_y.rearrange("p (g t) -> p g t", g=GROUPS),
                                        p_scale[:, :].unsqueeze(2).to_broadcast([P, GROUPS, P]),
                                        ALU.mult).then_inc(s_mixed, 1)

            def residual1(t):
                dve.wait_ge(s_o, OPEN + t + 1)
                dve.wait_ge(s_x1_free, OPEN + t)
                nc.vector.tensor_tensor(x1, ps_wide[:, :], mod[:, GATE1, :], ALU.mult).then_inc(s_x1, 1)
                dve.wait_ge(s_x1, OPEN + 2 * t + 1)
                dve.wait_ge(s_x_res, 16 * (t + 1))
                nc.vector.tensor_tensor(x1, x1, x_res, ALU.add).then_inc(s_x1, 1)

            norm1(0)
            norm1(1)
            layer_norm_v(0)
            with dve.Fori(1, TILES - 1) as t:
                mix(t - 1)
                norm1(t + 1)
                residual1(t - 1)
                layer_norm_v(t)
            mix(TILES - 2)
            residual1(TILES - 2)
            layer_norm_v(TILES - 1)
            mix(TILES - 1)
            residual1(TILES - 1)
            nc.vector.memset(ln_b[:, 0:HALF // 2], 0.0).then_inc(s_zeroed, 1)

            for s in range(SIDES):
                dve.wait_ge(s_fold, s + 1)
                nc.vector.tensor_copy(key_map[:, 4:8, s * KEYS:(s + 1) * KEYS],
                                      ps_fold[s % 2][:, HALF:D].rearrange("p (k n) -> p k n", k=4)).then_inc(s_fold_v, 1)

            def norm2(t):
                dve.wait_ge(s_ssq2, 2 * (t + 1))
                nc.vector.reciprocal(stat[:, 6:7], stat[:, 5:6]).then_inc(s_norm2, 1)
                dve.wait_ge(s_norm2, 2 * t + 1)
                nc.vector.scalar_tensor_tensor(out=h2_next[:, :], in0=x1_next[:, :], scalar=stat[:, 6:7],
                                               in1=mod[:, SCALE2, :], op0=ALU.mult, op1=ALU.mult).then_inc(s_norm2, 1)
                dve.wait_ge(s_norm2, 2 * t + 2)
                nc.vector.tensor_tensor(h2_next[:, :], h2_next[:, :], mod[:, SHIFT2, :], ALU.add).then_inc(s_h2, 1)

            def route_step(n, t, q):
                base = ROUTE_STEPS * (t * PAIRS + q)
                if n == 0:
                    dve.wait_ge(s_score_sb, OPEN + t * PAIRS + q + 1)
                    apart(dve)
                    for b in range(4):
                        last = nc.vector.max(top_s[:, b, 0:8], score[:, b, :])
                    last.then_inc(s_route, 1)
                    return
                dve.wait_ge(s_route, OPEN + base + n)
                if n in (1, 2, 3, 5, 6, 7, 8):
                    apart(dve)
                if n == 1:
                    for b in range(4):
                        nc.vector.max_index(top_i[:, b, 0:8], top_s[:, b, 0:8], score[:, b, :])
                        last = nc.vector.match_replace(score2[:, b, :], top_s[:, b, 0:8], score[:, b, :], LOWEST)
                elif n == 2:
                    for b in range(4):
                        last = nc.vector.max(top_s[:, b, 8:16], score2[:, b, :])
                elif n == 3:
                    for b in range(4):
                        last = nc.vector.max_index(top_i[:, b, 8:16], top_s[:, b, 8:16], score2[:, b, :])
                elif n == 4:
                    nc.vector.tensor_copy(top_f[:, :, :], top_i[:, :, :])
                    s_v4 = top_s[:, :, :].rearrange("p (h e) k -> p h e k", e=2)
                    for i in range(PAIR):
                        last = nc.vector.tensor_tensor(
                            cand[:, i, :].rearrange("p (a b) -> p a b", a=TOPK),
                            s_v4[:, i, 0, :].unsqueeze(2).to_broadcast([P, TOPK, TOPK]),
                            s_v4[:, i, 1, :].unsqueeze(1).to_broadcast([P, TOPK, TOPK]), ALU.add)
                elif n == 5:
                    for i in range(PAIR):
                        last = nc.vector.max(best[:, i, 0:8], cand[:, i, :])
                elif n == 6:
                    for i in range(PAIR):
                        nc.vector.max_index(sel[:, i, 0:8], best[:, i, 0:8], cand[:, i, :])
                        last = nc.vector.match_replace(cand2[:, i, :], best[:, i, 0:8], cand[:, i, :], LOWEST)
                elif n == 7:
                    for i in range(PAIR):
                        last = nc.vector.max(best[:, i, 8:16], cand2[:, i, :])
                elif n == 8:
                    for i in range(PAIR):
                        last = nc.vector.max_index(sel[:, i, 8:16], best[:, i, 8:16], cand2[:, i, :])
                elif n == 9:
                    nc.vector.tensor_single_scalar(sel_ab[:, 0, :, :], sel[:, :, :], 4, ALU.logical_shift_right)
                    nc.vector.tensor_single_scalar(sel_ab[:, 1, :, :], sel[:, :, :], TOPK - 1, ALU.bitwise_and)
                    last = nc.vector.tensor_tensor(
                        logits[:, bass.ds(q * TURN, TURN)].rearrange("p (h k) -> p h k", h=PAIR),
                        best[:, :, :], best[:, :, 0:1].to_broadcast([P, PAIR, TOPK]), ALU.subtract)
                elif n == 10:
                    last = nc.vector.tensor_copy(sel_f[:, :, :, :], sel_ab[:, :, :, :])
                elif n == 11:
                    for i in range(PAIR):
                        for e, onehot in enumerate((cand, cand2)):
                            last = nc.vector.tensor_tensor(
                                onehot[:, i, :].rearrange("p (k a) -> p k a", a=TOPK),
                                sel_f[:, e, i, :].unsqueeze(2).to_broadcast([P, TOPK, TOPK]),
                                iota16.unsqueeze(1).to_broadcast([P, TOPK, TOPK]), ALU.is_equal)
                elif n == 12:
                    for i in range(PAIR):
                        for e, onehot in enumerate((cand, cand2)):
                            v = onehot[:, i, :].rearrange("p (k a) -> p k a", a=TOPK)
                            last = nc.vector.tensor_tensor(
                                v, v, top_f[:, 2 * i + e, :].unsqueeze(1).to_broadcast([P, TOPK, TOPK]), ALU.mult)
                elif n == 13:
                    for e, onehot in enumerate((cand, cand2)):
                        last = nc.vector.tensor_reduce(
                            found[:, e, :, :].rearrange("p h k -> p (h k)"),
                            onehot[:, :, :].rearrange("p h (k a) -> p (h k) a", a=TOPK), AX_X, ALU.add)
                else:
                    dve.wait_ge(s_staged, (t - 1) * SLOTS // TOPK + (q + 1) * PAIR) if not isinstance(t, int) or t > 0 else None
                    last = nc.vector.scalar_tensor_tensor(
                        out=expert_rows[:, bass.ds(q * TURN, TURN)],
                        in0=found[:, 0, :, :].rearrange("p h k -> p (h k)"), scalar=float(KEYS),
                        in1=found[:, 1, :, :].rearrange("p h k -> p (h k)"), op0=ALU.mult, op1=ALU.add)
                last.then_inc(s_route, 1)

            def dot(turn, s):
                dve.wait_ge(s_row[s % RING], 16 * (turn * (TURN // RING) + s // RING + 1))
                down = ring[:, s % RING, 0:D]
                nc.vector.tensor_tensor_reduce(down, down, h2_cur, 1.0, 0.0,
                                                      ALU.mult, ALU.add, act_in[:, s:s + 1]).then_inc(s_dots, 1)

            def softmax(t):
                dve.wait_ge(s_exp, t + 1)
                e_v = expd[:, :].rearrange("p (h k) -> p h k", h=HEADS)
                nc.vector.tensor_reduce(sums[:, 0, :], e_v, AX_X, ALU.add).then_inc(s_soft, 1)
                dve.wait_ge(s_soft, 3 * t + 1)
                nc.vector.reciprocal(sums[:, 1, :], sums[:, 0, :]).then_inc(s_soft, 1)
                dve.wait_ge(s_soft, 3 * t + 2)
                nc.vector.tensor_tensor(gate[:, :].rearrange("p (h k) -> p h k", h=HEADS), e_v,
                                        sums[:, 1, :].unsqueeze(2).to_broadcast([P, HEADS, TOPK]),
                                        ALU.mult).then_inc(s_soft, 1)
                dve.wait_ge(s_tr2, 2 * (t + 1))
                nc.vector.tensor_copy(h2_cur, h2_next[:, :]).then_inc(s_h2c, 1)

            def finish(t):
                dve.wait_ge(s_sum, t + 1)
                dve.wait_ge(s_y_free, OPEN + t)
                nc.vector.tensor_tensor(y, ps_sum[:, :], mod[:, GATE2, :], ALU.mult).then_inc(s_fin, 1)
                dve.wait_ge(s_fin, OPEN + 4 * t + 1)
                dve.wait_ge(s_x1f, 16 * (t + 1))
                nc.vector.tensor_tensor(y, y, x1_fin, ALU.add).then_inc(s_fin, 1)
                dve.wait_ge(s_ssq3, 2 * (t + 1))
                nc.vector.reciprocal(stat[:, 10:11], stat[:, 9:10]).then_inc(s_rms, 1)
                dve.wait_ge(s_rms, t + 1)
                nc.vector.scalar_tensor_tensor(out=y, in0=y, scalar=stat[:, 10:11], in1=gf[:, :],
                                               op0=ALU.mult, op1=ALU.mult).then_inc(s_fin, 2)

            def tile_turns(t, route, expert):
                if route:
                    norm2(t)
                with dve.Fori(0, PAIRS) as q:
                    turn = (t - 1) * PAIRS + q
                    if expert:
                        dve.wait_ge(s_h2c, t)
                    if not expert:
                        for n in range(ROUTE_STEPS):
                            route_step(n, t, q)
                    else:
                        for s in range(TURN):
                            dot(turn, s)
                            if route and s % 2 == 1 and s > 1:
                                route_step(s // 2 - 1, t, q)
                if route:
                    softmax(t)
                if expert:
                    finish(t - 1)

            tile_turns(0, True, False)
            with dve.Fori(1, TILES) as t:
                tile_turns(t, True, True)
            tile_turns(TILES, False, True)


def kernel(x, c, w_ada, b_ada, g_norm1, w_in, w_pool, pool_scale, sgu_ln_g, sgu_ln_b, w_spatial, b_spatial,
           w_out, g_norm2, w_query, sub_keys, expert_down, expert_up, g_final):
    import concourse.bacc as bacc
    from concourse.bass_utils import run_bass_kernel_spmd

    rows = np.ascontiguousarray
    arrays = {
        "x": rows(x), "c": rows(c), "w_ada": rows(w_ada), "b_ada": rows(b_ada).reshape(-1),
        "g_norm1": rows(g_norm1).reshape(-1), "w_in": rows(w_in), "w_pool": rows(w_pool),
        "pool_scale": rows(np.asarray(pool_scale).reshape(GROUPS, P).T),
        "sgu_ln_g": rows(sgu_ln_g).reshape(-1), "sgu_ln_b": rows(sgu_ln_b).reshape(-1),
        "w_spatial_t": rows(np.transpose(np.asarray(w_spatial)[0], (2, 0, 1))).reshape(P, GROUPS * P),
        "b_spatial": rows(b_spatial).reshape(-1),
        "w_out": rows(w_out), "g_norm2": rows(g_norm2).reshape(-1),
        "w_query_t": rows(np.transpose(np.asarray(w_query)[0].reshape(D, SIDES, P), (2, 1, 0))),
        "sub_keys_t": rows(np.transpose(np.asarray(sub_keys)[0].reshape(SIDES, KEYS, P), (2, 0, 1))),
        "experts": np.concatenate([np.asarray(expert_down)[0], np.asarray(expert_up)[0]], axis=1),
        "g_final": rows(g_final).reshape(-1),
        "constants": shape_constants(),
    }
    nc = bacc.Bacc("TRN2", target_bir_lowering=False, num_devices=1)
    handles = [nc.dram_tensor(name, a.shape, F32, kind="ExternalInput").ap() for name, a in arrays.items()]
    x1_dram = nc.dram_tensor("x1_scratch", (TILES, P, D), F32).ap()
    out = nc.dram_tensor("out", (1, SEQ, D), F32, kind="ExternalOutput").ap()
    build(nc, *handles, x1_dram, out)
    result = run_bass_kernel_spmd(nc, [arrays], core_ids=[0])
    return result.results[0]["out"]
```

```python
from contextlib import ExitStack

import numpy as np
import concourse.bass as bass
from concourse import mybir

F32 = mybir.dt.float32
U32 = mybir.dt.uint32
BF16 = mybir.dt.bfloat16
ALU = mybir.AluOpType
ACT = mybir.ActivationFunctionType
AX_X = mybir.AxisListType.X

P = 128
D = 1024
SEQ = 1024
TILES = SEQ // P
KC = D // P
HALF = 512
POOL_WINDOWS = (2, 4, 8, 16)
GROUPS = len(POOL_WINDOWS)
IN_WIDTH = 3 * HALF
N_MOD = 6
HEADS = 8
SIDES = 2 * HEADS
KEYS = 128
TOPK = 16
SLOTS = HEADS * TOPK
EPS = 1e-6
LOWEST = -3.0e38

PAIR = 2
PAIRS = HEADS // PAIR
RING = 8
TURN = PAIR * TOPK
ROWS_STEP = 15
ROUTE_STEPS = 18
COPY_SLOT = 2
ROUTE_SLOT = 3
EXP_SLOT = 18
GATE_SLOT = 22
EARLY = 6
OPEN = 1

C_IDENT = 0
C_FIRST = P
C_BAND = C_FIRST + GROUPS * P
C_PREV = C_BAND + GROUPS * P
C_TRIL = C_PREV + GROUPS * P
C_IOTA = C_TRIL + P
C_EPS = C_IOTA + TOPK
C_ALL = C_EPS + 1


def shape_constants():
    out = np.zeros((P, C_ALL), np.float32)
    out[:, C_IDENT:C_IDENT + P] = np.eye(P)
    s, t = np.arange(P)[:, None], np.arange(P)[None, :]
    for g, w in enumerate(POOL_WINDOWS):
        near = (s <= t) & (s > t - w)
        eye = (s == t).astype(np.float32)
        out[:, C_FIRST + g * P:C_FIRST + (g + 1) * P] = near / np.minimum(t + 1.0, w) - eye
        out[:, C_BAND + g * P:C_BAND + (g + 1) * P] = near / float(w) - eye
        out[:, C_PREV + g * P:C_PREV + (g + 1) * P] = (s - P > t - w) / float(w)
    out[:, C_TRIL:C_TRIL + P] = s <= t
    out[:, C_IOTA:C_EPS] = np.arange(TOPK)
    out[:, C_EPS] = EPS
    return out


def build(nc, x, c, w_ada, b_ada, g_norm1, w_in, w_pool, pool_scale, sgu_ln_g, sgu_ln_b, w_spatial_t,
          b_spatial, w_out, g_norm2, w_query_t, sub_keys_t, experts, g_final, constants, x1_dram, out):
    with ExitStack() as ctx:
        def sb(name, shape, dt=F32):
            return ctx.enter_context(nc.sbuf_tensor(name, shape, dt))

        def sem(name):
            return ctx.enter_context(nc.semaphore(name))

        region_a = sb("region_a", [P, 20 * 1024])
        w_in_sb = region_a[:, 0:KC * IN_WIDTH].rearrange("p (k n) -> p k n", k=KC)
        w_out_sb = region_a[:, KC * IN_WIDTH:KC * (IN_WIDTH + D)].rearrange("p (k n) -> p k n", k=KC)
        wq_t = region_a[:, 0:SIDES * D].rearrange("p (s d) -> p s d", s=SIDES)
        keys_t = region_a[:, SIDES * D:SIDES * D + SIDES * KEYS].rearrange("p (s k) -> p s k", s=SIDES)
        ring = region_a[:, 0:RING * 2 * D].rearrange("p (r n) -> p r n", r=RING)
        SPARE = RING * 2 * D
        h2_cur = region_a[:, SPARE:SPARE + D]
        squares = region_a[:, SPARE + D:SPARE + 2 * D]
        x1_fin = region_a[:, SPARE + 2 * D:SPARE + 3 * D]
        y = region_a[:, SPARE + 3 * D:SPARE + 4 * D]

        region_b = sb("region_b", [P, 16 * 1024])
        key_map = region_b[:, :].rearrange("p (k n) -> p k n", k=KC)
        ADA_W = KC * HALF
        ada_stage = [region_b[:, (2 + i) * ADA_W:(3 + i) * ADA_W].rearrange("p (k n) -> p k n", k=KC)
                     for i in range(2)]
        at = [0]

        def temp(n):
            at[0] += n
            assert at[0] <= 2 * ADA_W
            return region_b[:, at[0] - n:at[0]]

        x_in = temp(D)
        x_res = temp(D)
        h = temp(D)
        h_t = temp(D).rearrange("p (k t) -> p k t", k=KC)
        mixed_t = temp(D).rearrange("p (k t) -> p k t", k=KC)
        vn = temp(HALF)
        u_t = temp(HALF)
        pooled_t = temp(HALF)
        gated = temp(HALF)
        a_prev = temp(HALF)
        a_cur = temp(HALF)

        mod = sb("mod", [P, N_MOD, D])
        mod_rows = mod[:, :, :].rearrange("p m d -> p (m d)")
        SHIFT1, SCALE1, GATE1, SHIFT2, SCALE2, GATE2 = range(N_MOD)
        gf = sb("gf", [P, D])
        const = sb("const", [P, C_ALL])
        ident = const[:, C_IDENT:C_IDENT + P]
        band_cur = const[:, C_FIRST:C_FIRST + GROUPS * P]
        band_gen = const[:, C_BAND:C_BAND + GROUPS * P]
        band_prev = const[:, C_PREV:C_PREV + GROUPS * P]
        tril_t = const[:, C_TRIL:C_TRIL + P]
        iota16 = const[:, C_IOTA:C_IOTA + TOPK]
        eps = const[:, C_EPS:C_EPS + 1]
        small_w = sb("small_w", [P, 4 * HALF])
        w_pool_sb = small_w[:, 0:HALF]
        w_sp_t = small_w[:, HALF:2 * HALF]
        b_sp = small_w[:, 2 * HALF:3 * HALF]
        ln_g = small_w[:, 3 * HALF:4 * HALF]
        ln_b = sb("ln_b", [P, HALF])
        p_scale = sb("p_scale", [P, GROUPS])
        c_cols = sb("c_cols", [P, KC])
        c_act = sb("c_act", [P, KC])

        x1_next = sb("x1_next", [P, D])
        h2_next = sb("h2_next", [P, D])
        h2_t = sb("h2_t", [P, KC, P])
        ones = h2_t[:, 0, :]
        ada_sum = [h2_t[:, 1:5, :].rearrange("p k t -> p (k t)"),
                   mixed_t[:, 0:4, :].rearrange("p k t -> p (k t)")]
        g1, g2 = x1_next, h2_next
        diag = sb("diag", [P, RING, P])
        x1 = diag[:, :, :].rearrange("p r t -> p (r t)")

        score = small_w[:, 0:HALF].rearrange("p (b k) -> p b k", b=4)
        cand = small_w[:, HALF:2 * HALF].rearrange("p (h k) -> p h k", h=PAIR)
        cand2 = small_w[:, 2 * HALF:3 * HALF].rearrange("p (h k) -> p h k", h=PAIR)
        score2 = small_w[:, 2 * HALF:3 * HALF].rearrange("p (b k) -> p b k", b=4)
        logits, expd = (small_w[:, 3 * HALF + i * SLOTS:3 * HALF + i * SLOTS + TURN] for i in range(2))
        exp_v = expd.rearrange("p (h k) -> p h k", h=PAIR)
        gate = small_w[:, 3 * HALF + 2 * SLOTS:3 * HALF + 3 * SLOTS]
        act_in, act_out, weight = (small_w[:, 3 * HALF + 3 * SLOTS + i * TURN:3 * HALF + 3 * SLOTS + (i + 1) * TURN]
                                   for i in range(3))
        top_s, top_f = (band_cur[:, i * 4 * TOPK:(i + 1) * 4 * TOPK].rearrange("p (b k) -> p b k", b=4)
                        for i in range(2))
        sel_f, found = (band_gen[:, i * 2 * TURN:(i + 1) * 2 * TURN].rearrange("p (e h k) -> p e h k", e=2, h=PAIR)
                        for i in range(2))
        best = band_prev[:, 0:TURN].rearrange("p (h k) -> p h k", h=PAIR)
        top_i = sb("top_i", [P, 4, TOPK], U32)
        sel = sb("sel", [P, PAIR, TOPK], U32)
        sel_ab = sb("sel_ab", [P, 2, PAIR, TOPK], U32)
        expert_rows = sb("expert_rows", [P, SLOTS], U32)
        row_stage = [sb(f"row_stage{i}", [P, TOPK], U32) for i in range(PAIR)]
        stat = sb("stat", [P, 16])
        v_stats = sb("v_stats", [P, 6])
        v_mean_var = sb("v_mean_var", [P, 2])
        sums = sb("sums", [P, 2, PAIR])
        zero_bf = ln_b[:, 0:HALF // 2].bitcast(BF16)

        banks = [ctx.enter_context(nc.psum_tensor(f"banks{i}", [P, D], F32)) for i in range(4)]
        ps_wide = banks[0]
        ps_v, ps_a = banks[1][:, 0:HALF], banks[1][:, HALF:D]
        ps_u, ps_pool = banks[2][:, 0:HALF], banks[2][:, HALF:D]
        ps_y, ps_sgu = banks[3][:, 0:HALF], banks[3][:, HALF:D]
        ps_ada = [banks[3][:, 0:HALF], banks[3][:, HALF:D]]
        ps_fold = [banks[1], banks[2]]
        ps_h2 = banks[1]
        ps_score = banks[2][:, 0:HALF]
        ps_sum = banks[0]

        s_const = sem("const_loaded")
        s_b_ada = sem("b_ada_loaded")
        s_g1 = sem("g_norm1_loaded")
        s_rows = sem("g_norm2_g_final_loaded")
        s_small = sem("small_weights_loaded")
        s_ada_w = [sem("ada_stage0_loaded"), sem("ada_stage1_loaded")]
        s_w_in = [sem(f"w_in_{n}_loaded") for n in "vau"]
        s_w_out = sem("w_out_loaded")
        s_x_in = sem("x_in_loaded")
        s_x_res = sem("x_res_loaded")
        s_cact = sem("c_act_ready")
        s_ones = sem("ones_ready")
        s_acc = sem("ada_sum_steps")
        s_ada_ps = sem("ada_psum_ready")
        s_mod = sem("mod_rows_ready")
        s_scales = sem("scales_folded")
        s_masked = sem("w_spatial_masked")
        s_init = sem("start_values_set")
        s_ssq1 = sem("ssq1_ready")
        s_norm1 = sem("norm1_steps")
        s_h = sem("h_ready")
        s_tr = sem("h_transposed")
        s_ht = sem("h_t_ready")
        s_v = sem("v_psum_ready")
        s_a = sem("a_psum_ready")
        s_u = sem("u_psum_ready")
        s_ln = sem("ln_steps")
        s_v_root = sem("v_root_ready")
        s_a_sb = sem("a_ready")
        s_u_sb = sem("u_t_ready")
        s_pool = sem("pool_psum_ready")
        s_turned = sem("pool_state_turned")
        s_pooled = sem("pooled_ready")
        s_y = sem("y_psum_ready")
        s_sgu = sem("sgu_psum_ready")
        s_gated = sem("gated_ready")
        s_mixed = sem("mixed_ready")
        s_o = sem("out_psum_ready")
        s_x1 = sem("x1_steps")
        s_x1_st = sem("x1_stored")
        s_x1_free = sem("x1_free")
        s_wq = [sem(f"w_query{n}_loaded") for n in range(4)]
        s_keys = sem("keys_loaded")
        s_fold = sem("fold_psum_ready")
        s_fold_a = sem("key_map_by_act")
        s_fold_v = sem("key_map_by_vector")
        s_x1n = sem("x1_next_loaded")
        s_ssq2 = sem("ssq2_ready")
        s_norm2 = sem("norm2_steps")
        s_h2 = sem("h2_ready")
        s_tr2 = sem("h2_transposed")
        s_h2t = sem("h2_t_ready")
        s_score = sem("score_psum_ready")
        s_score_sb = sem("score_ready")
        s_route = sem("route_steps")
        s_staged = sem("rows_staged")
        s_exp = sem("exp_ready")
        s_h2c = sem("h2_cur_ready")
        s_row = [sem(f"expert_row{r}_landed") for r in range(RING)]
        s_free = sem("ring_slots_free")
        s_dots = sem("dots_ready")
        s_gelu = sem("gelu_ready")
        s_weight = sem("weights_ready")
        s_diag = sem("diags_ready")
        s_zeroed = sem("sums_zeroed")
        s_sum = sem("sums_ready")
        s_fin = sem("final_steps")
        s_ssq3 = sem("ssq3_ready")
        s_rms = sem("final_norm_steps")
        s_x1f = sem("x1_final_loaded")
        s_out = sem("out_stored")
        s_y_free = sem("y_free")

        x_v = x.rearrange("b (t p) d -> (b t) p d", p=P)
        out_v = out.rearrange("b (t p) d -> (b t) p d", p=P)
        ada_v = w_ada.rearrange("l (p k) n -> (l p) k n", k=KC)
        w_in_v = w_in.rearrange("l (k p) n -> p (l k) n", p=P)
        w_out_v = w_out.rearrange("l (k p) n -> p (l k) n", p=P)

        block = ctx.enter_context(nc.Block())

        def spread(row, n):
            return row.rearrange("a n -> (a n)")[0:n].partition_broadcast(P)

        def apart(engine):
            engine.nop(nofuse=True)

        def mod_before(t):
            return 2 * N_MOD if isinstance(t, int) and t > TILES - 2 else EARLY + t

        @block.sync
        def _(sp):
            sp.sem_inc(s_x1_free, OPEN)
            sp.sem_inc(s_y_free, OPEN)
            sp.dma_start(c_cols[:, :], c.rearrange("b (p k) -> (b p) k", k=KC)).then_inc(s_const, 16)
            sp.dma_start(const[:, :], constants).then_inc(s_const, 16)

            def load_ada(j):
                if j >= 2:
                    sp.wait_ge(s_acc, KC * (j - 1))
                sp.dma_start(ada_stage[j % 2], ada_v[:, :, j * HALF:(j + 1) * HALF]).then_inc(s_ada_w[j % 2], 16)

            def load_ada_late(t):
                sp.wait_ge(s_acc, KC * (EARLY - 1 + t))
                sp.dma_start(ada_stage[0], ada_v[:, :, bass.ds((EARLY - 1 + t) * HALF, HALF)]).then_inc(s_ada_w[0], 16)

            load_ada(0)
            load_ada(1)
            sp.dma_start(mod[0:1, :, :].rearrange("p m d -> p (m d)"), b_ada.unsqueeze(0)).then_inc(s_b_ada, 16)
            sp.dma_start(g1[:, :], g_norm1.partition_broadcast(P)).then_inc(s_g1, 16)
            sp.dma_start(x_in, x_v[0]).then_inc(s_x_in, 16)
            load_ada(2)
            load_ada(3)
            for n, col in enumerate((2 * HALF, 0, HALF)):
                sp.dma_start(w_in_sb[:, :, col:col + HALF], w_in_v[:, :, col:col + HALF]).then_inc(s_w_in[n], 16)
            sp.dma_start(w_sp_t, w_spatial_t).then_inc(s_small, 16)
            sp.dma_start(ln_g, sgu_ln_g.partition_broadcast(P)).then_inc(s_small, 16)
            sp.dma_start(ln_b[:, :], sgu_ln_b.partition_broadcast(P)).then_inc(s_small, 16)
            load_ada(4)
            load_ada(5)
            sp.dma_start(w_pool_sb.rearrange("p (g d) -> p g d", g=GROUPS),
                         w_pool.rearrange("l g c d -> c (l g) d")).then_inc(s_small, 16)
            sp.dma_start(b_sp, b_spatial.partition_broadcast(P)).then_inc(s_small, 16)
            sp.dma_start(p_scale[:, :], pool_scale).then_inc(s_small, 16)
            sp.dma_start(w_out_sb, w_out_v).then_inc(s_w_out, 16)

            def mixer_loads(t):
                sp.wait_ge(s_norm1, 2 * t)
                sp.dma_start(x_in, x_v[t]).then_inc(s_x_in, 16)
                if not isinstance(t, int) or t >= 2:
                    sp.wait_ge(s_x1, OPEN + 2 * (t - 1))
                sp.dma_start(x_res, x_v[t - 1]).then_inc(s_x_res, 16)

            def store_x1(t):
                sp.wait_ge(s_x1, OPEN + 2 * (t + 1))
                sp.dma_start(x1_dram[t], x1).then_inc(s_x1_st, 16)
                sp.wait_ge(s_x1_st, 16 * (t + 1))
                sp.sem_inc(s_x1_free, 1)

            mixer_loads(1)
            load_ada_late(1)
            sp.dma_start(g2[:, :], g_norm2.partition_broadcast(P)).then_inc(s_rows, 16)
            sp.dma_start(gf[:, :], g_final.partition_broadcast(P)).then_inc(s_rows, 16)
            with sp.Fori(2, TILES - 1) as t:
                mixer_loads(t)
                load_ada_late(t)
                store_x1(t - 2)
            mixer_loads(TILES - 1)
            store_x1(TILES - 3)
            sp.wait_ge(s_x1, OPEN + 2 * (TILES - 1))
            sp.dma_start(x_res, x_v[TILES - 1]).then_inc(s_x_res, 16)
            store_x1(TILES - 2)

            sp.wait_ge(s_u, TILES)
            in_w_in = KC * IN_WIDTH // D
            wq_v = w_query_t
            for n in range(3):
                a, b = n * in_w_in // 3, (n + 1) * in_w_in // 3
                sp.dma_start(wq_t[:, a:b, :], wq_v[:, a:b, :]).then_inc(s_wq[n], 16)
            sp.wait_ge(s_o, OPEN + TILES)
            sp.dma_start(keys_t, sub_keys_t).then_inc(s_keys, 16)
            sp.dma_start(wq_t[:, in_w_in:SIDES, :], wq_v[:, in_w_in:SIDES, :]).then_inc(s_wq[3], 16)
            store_x1(TILES - 1)

            sp.wait_ge(s_scales, 2)
            sp.dma_start(x1_next[:, :], x1_dram[0]).then_inc(s_x1n, 16)

            def expert_loads(t, last):
                sp.wait_ge(s_fin, OPEN + 4 * t)
                sp.dma_start(x1_fin, x1_dram[t]).then_inc(s_x1f, 16)
                if not last:
                    sp.wait_ge(s_norm2, 2 * (t + 1))
                    sp.dma_start(x1_next[:, :], x1_dram[t + 1]).then_inc(s_x1n, 16)
                sp.wait_ge(s_fin, OPEN + 4 * (t + 1))
                sp.dma_start(out_v[t], y).then_inc(s_out, 16)
                sp.wait_ge(s_out, 16 * (t + 1))
                sp.sem_inc(s_y_free, 1)

            sp.wait_ge(s_h2c, 1)
            with sp.Fori(0, TILES - 1) as t:
                expert_loads(t, False)
            expert_loads(TILES - 1, True)

        @block.gpsimd
        def _(pool):
            pool.sem_inc(s_turned, OPEN)
            nc.gpsimd.memset(a_prev, 0.0).then_inc(s_init, 1)

            def turn_pool_state(t):
                pool.wait_ge(s_pool, t + 1)
                apart(pool)
                nc.gpsimd.tensor_copy(a_prev, a_cur)
                nc.gpsimd.tensor_copy(band_cur, band_gen).then_inc(s_turned, 1)

            with pool.Fori(0, TILES - 1) as t:
                turn_pool_state(t)

            def gather_turn(t, q):
                turn = t * PAIRS + q
                for i in range(PAIR):
                    pool.wait_ge(s_route, OPEN + ROUTE_STEPS * turn + ROWS_STEP)
                    pool.wait_ge(s_free, turn * TURN + i * TOPK + 1)
                    apart(pool)
                    nc.gpsimd.tensor_copy(row_stage[i][:, :],
                                          expert_rows[:, bass.ds((q * PAIR + i) * TOPK, TOPK)]).then_inc(s_staged, 1)
                    pool.wait_ge(s_staged, turn * PAIR + i + 1)
                    for k in range(TOPK):
                        s = i * TOPK + k
                        pool.wait_ge(s_free, turn * TURN + s + 1)
                        apart(pool)
                        nc.gpsimd.indirect_dma_start(
                            ring[:, s % RING, :], None, experts,
                            bass.IndirectOffsetOnAxis(ap=row_stage[i][:, k:k + 1], axis=0),
                        ).then_inc(s_row[s % RING], 16)

            pool.wait_ge(s_fold, SIDES)
            with pool.Fori(0, TILES) as t:
                with pool.Fori(0, PAIRS) as q:
                    gather_turn(t, q)

        @block.tensor
        def _(pe):
            pe.sem_inc(s_y, OPEN)
            pe.sem_inc(s_o, OPEN)
            def spread_ada(row, total, bank):
                nc.tensor.matmul(bank, ones, total, start=True, stop=False)
                nc.tensor.matmul(bank, ones[0:1, :], row, start=False, stop=True).then_inc(s_ada_ps, 1)

            def spread_early(j):
                pe.wait_ge(s_acc, KC * (j + 1))
                if j >= 2:
                    pe.wait_ge(s_mod, j - 1)
                spread_ada(mod[0:1, j // 2, (j % 2) * HALF:(j % 2 + 1) * HALF], ada_sum[j % 2], ps_ada[j % 2])

            def spread_late(t):
                pe.wait_ge(s_acc, KC * (EARLY + t))
                pe.wait_ge(s_mixed, 2 * t)
                spread_ada(mod_rows[0:1, bass.ds((EARLY - 1 + t) * HALF, HALF)], ada_sum[0], ps_y)

            pe.wait_ge(s_ones, 1)
            pe.wait_ge(s_b_ada, 16)
            for j in range(4):
                spread_early(j)

            def transposes(t):
                pe.wait_ge(s_h, t + 1)
                for k in range(KC):
                    last = nc.tensor.transpose(ps_wide[:, k * P:(k + 1) * P], h[:, k * P:(k + 1) * P], ident)
                    if k % 4 == 3:
                        last.then_inc(s_tr, 1)

            def projection(t):
                pe.wait_ge(s_ht, 2 * (t + 1))
                if isinstance(t, int) and t == 0:
                    pe.wait_ge(s_w_in[0], 16)
                for k in range(KC):
                    last = nc.tensor.matmul(ps_v, h_t[:, k, :], w_in_sb[:, k, 2 * HALF:3 * HALF],
                                            start=(k == 0), stop=(k == KC - 1))
                last.then_inc(s_v, 1)
                if isinstance(t, int) and t == 0:
                    pe.wait_ge(s_w_in[1], 16)
                for k in range(KC):
                    last = nc.tensor.matmul(ps_a, h_t[:, k, :], w_in_sb[:, k, 0:HALF],
                                            start=(k == 0), stop=(k == KC - 1))
                last.then_inc(s_a, 1)
                if isinstance(t, int) and t == 0:
                    pe.wait_ge(s_w_in[2], 16)
                for g in range(GROUPS):
                    for k in range(KC):
                        last = nc.tensor.matmul(ps_u[:, g * P:(g + 1) * P],
                                                w_in_sb[:, k, HALF + g * P:HALF + (g + 1) * P], h_t[:, k, :],
                                                start=(k == 0), stop=(k == KC - 1))
                last.then_inc(s_u, 1)

            def mix(t):
                pe.wait_ge(s_a_sb, t + 1)
                pe.wait_ge(s_turned, OPEN + t)
                for g in range(GROUPS):
                    cols = slice(g * P, (g + 1) * P)
                    nc.tensor.matmul(ps_pool[:, cols], a_cur[:, cols], band_cur[:, cols], start=True, stop=False)
                    last = nc.tensor.matmul(ps_pool[:, cols], a_prev[:, cols], band_prev[:, cols],
                                            start=False, stop=True)
                last.then_inc(s_pool, 1)
                pe.wait_ge(s_ln, 6 * (t + 1))
                for g in range(GROUPS):
                    cols = slice(g * P, (g + 1) * P)
                    last = nc.tensor.matmul(ps_sgu[:, cols], vn[:, cols], w_sp_t[:, cols], start=True, stop=True)
                last.then_inc(s_sgu, 1)
                pe.wait_ge(s_pooled, t + 1)
                pe.wait_ge(s_mod, mod_before(t))
                for g in range(GROUPS):
                    cols = slice(g * P, (g + 1) * P)
                    last = nc.tensor.matmul(ps_y[:, cols], w_pool_sb[:, cols], pooled_t[:, cols], start=True, stop=True)
                last.then_inc(s_y, 1)
                pe.wait_ge(s_mixed, 2 * (t + 1))
                for n in range(2):
                    for i, k in enumerate([*range(GROUPS, KC), *range(GROUPS)]):
                        last = nc.tensor.matmul(ps_wide[:, n * HALF:(n + 1) * HALF], mixed_t[:, k, :],
                                                w_out_sb[:, k, n * HALF:(n + 1) * HALF],
                                                start=(i == 0), stop=(i == KC - 1))
                last.then_inc(s_o, 1)

            transposes(0)
            projection(0)
            spread_early(4)
            spread_early(5)
            pe.wait_ge(s_small, 96)
            pe.wait_ge(s_masked, 1)
            pe.wait_ge(s_init, 1)
            pe.wait_ge(s_w_out, 16)

            def mixer_iteration(t):
                pe.wait_ge(s_x1, OPEN + 2 * (t - 1))
                transposes(t)
                mix(t - 1)
                projection(t)

            with pe.Fori(1, TILES - 1) as t:
                mixer_iteration(t)
                spread_late(t)
            mixer_iteration(TILES - 1)
            mix(TILES - 1)

            pe.wait_ge(s_keys, 16)
            for s in range(SIDES):
                pe.wait_ge(s_wq[s // 4], 16)
                if s >= 2:
                    pe.wait_ge(s_fold_a, s - 1)
                    pe.wait_ge(s_fold_v, s - 1)
                for k in range(KC):
                    last = nc.tensor.matmul(ps_fold[s % 2][:, k * KEYS:(k + 1) * KEYS],
                                            wq_t[:, s, k * P:(k + 1) * P], keys_t[:, s, :], start=True, stop=True)
                last.then_inc(s_fold, 1)

            def transposes2(t):
                pe.wait_ge(s_h2, t + 1)
                for k in range(KC):
                    last = nc.tensor.transpose(ps_h2[:, k * P:(k + 1) * P], h2_next[:, k * P:(k + 1) * P], ident)
                    if k % 4 == 3:
                        last.then_inc(s_tr2, 1)

            def scores(t, q):
                pe.wait_ge(s_h2t, 2 * (t + 1))
                pe.wait_ge(s_score_sb, OPEN + t * PAIRS + q)
                for k in range(KC):
                    last = nc.tensor.matmul(ps_score, h2_t[:, k, :], key_map[:, k, bass.ds(q * 4 * KEYS, 4 * KEYS)],
                                            start=(k == 0), stop=(k == KC - 1))
                last.then_inc(s_score, 1)

            def clear_sums(stop):
                for n in range(2):
                    last = nc.tensor.matmul(ps_sum[:, n * HALF:(n + 1) * HALF], zero_bf[:, 0:P], zero_bf,
                                     start=not stop, stop=stop, skip_group_check=True)
                return last

            def add_expert(turn, s):
                pe.wait_ge(s_diag, turn * TURN + s + 1)
                for n in range(2):
                    last = nc.tensor.matmul(ps_sum[:, n * HALF:(n + 1) * HALF], diag[:, s % RING, :],
                                            ring[:, s % RING, D + n * HALF:D + (n + 1) * HALF],
                                            start=False, stop=False, skip_group_check=True)
                last.then_inc(s_free, 1)

            pe.wait_ge(s_fold_a, SIDES)
            pe.wait_ge(s_fold_v, SIDES)
            pe.wait_ge(s_zeroed, 1)
            pe.sem_inc(s_free, RING)

            def expert_turn(t, q):
                for s in range(TURN):
                    add_expert(t * PAIRS + q, s)

            def expert_tile(t, last):
                pe.wait_ge(s_fin, OPEN + 4 * t)
                clear_sums(False)
                with pe.Fori(0, PAIRS - 1) as q:
                    scores(t, q + 1)
                    expert_turn(t, q)
                if not last:
                    transposes2(t + 1)
                    scores(t + 1, 0)
                expert_turn(t, PAIRS - 1)
                clear_sums(True).then_inc(s_sum, 1)

            transposes2(0)
            scores(0, 0)
            with pe.Fori(0, TILES - 1) as t:
                expert_tile(t, False)
            expert_tile(TILES - 1, True)

        @block.scalar
        def _(act):
            act.sem_inc(s_score_sb, OPEN)
            act.wait_ge(s_const, 32)
            nc.scalar.activation(c_act[:, :], c_cols[:, :], ACT.Silu).then_inc(s_cact, 1)

            def root(mean_sq, out_col, steps, base, scale):
                act.wait_ge(steps, base + 1)
                nc.scalar.activation(out_col, mean_sq, ACT.Sqrt, bias=eps, scale=scale).then_inc(steps, 1)

            def square1(t):
                act.wait_ge(s_x_in, 16 * (t + 1))
                act.wait_ge(s_tr, 2 * t)
                nc.scalar.activation(h, x_in, ACT.Square, accum_out=stat[:, 0:1]).then_inc(s_ssq1, 1)
                root(stat[:, 0:1], stat[:, 1:2], s_ssq1, 2 * t, 1.0 / D)

            def copy_h_t(t):
                for n in range(2):
                    act.wait_ge(s_tr, 2 * t + n + 1)
                    act.wait_ge(s_u, t)
                    nc.scalar.copy(h_t[:, 4 * n:4 * n + 4, :].rearrange("p k t -> p (k t)"),
                                   ps_wide[:, n * HALF:(n + 1) * HALF]).then_inc(s_ht, 1)

            def copy_pooled(t):
                act.wait_ge(s_pool, t + 1)
                act.wait_ge(s_y, OPEN + t)
                nc.scalar.copy(pooled_t, ps_pool).then_inc(s_pooled, 1)

            def copy_a_u(t):
                act.wait_ge(s_ln, 6 * t + 2)
                nc.scalar.activation(stat[:, 12:13], v_mean_var[:, 1:2], ACT.Sqrt, bias=eps).then_inc(s_v_root, 1)
                act.wait_ge(s_a, t + 1)
                act.wait_ge(s_turned, OPEN + t)
                nc.scalar.copy(a_cur, ps_a).then_inc(s_a_sb, 1)
                act.wait_ge(s_u, t + 1)
                act.wait_ge(s_mixed, 2 * t)
                nc.scalar.copy(u_t, ps_u).then_inc(s_u_sb, 1)

            square1(0)
            copy_h_t(0)
            square1(1)
            copy_a_u(0)
            with act.Fori(1, TILES - 1) as t:
                copy_h_t(t)
                copy_pooled(t - 1)
                square1(t + 1)
                copy_a_u(t)
            copy_h_t(TILES - 1)
            copy_pooled(TILES - 2)
            copy_a_u(TILES - 1)
            copy_pooled(TILES - 1)

            act.wait_ge(s_o, OPEN + TILES)
            act.wait_ge(s_gated, TILES)
            act.wait_ge(s_x1, OPEN + 2 * TILES)
            act.wait_ge(s_mixed, 2 * TILES)
            for s in range(SIDES):
                act.wait_ge(s_fold, s + 1)
                nc.scalar.copy(key_map[:, 0:4, s * KEYS:(s + 1) * KEYS],
                               ps_fold[s % 2][:, 0:HALF].rearrange("p (k n) -> p k n", k=4)).then_inc(s_fold_a, 1)

            def square2(t):
                act.wait_ge(s_x1n, 16 * (t + 1))
                if not isinstance(t, int) or t > 0:
                    act.wait_ge(s_h2c, t)
                nc.scalar.activation(h2_next[:, :], x1_next[:, :], ACT.Square,
                                     accum_out=stat[:, 4:5]).then_inc(s_ssq2, 1)
                root(stat[:, 4:5], stat[:, 5:6], s_ssq2, 2 * t, 1.0 / D)

            def copy_h2_t(t):
                for n in range(2):
                    act.wait_ge(s_tr2, 2 * t + n + 1)
                    nc.scalar.copy(h2_t[:, 4 * n:4 * n + 4, :].rearrange("p k t -> p (k t)"),
                                   ps_h2[:, n * HALF:(n + 1) * HALF]).then_inc(s_h2t, 1)

            def copy_score(t, q):
                turn = t * PAIRS + q
                act.wait_ge(s_score, turn + 1)
                act.wait_ge(s_route, OPEN + ROUTE_STEPS * turn)
                nc.scalar.copy(score[:, :, :].rearrange("p b k -> p (b k)"), ps_score).then_inc(s_score_sb, 1)

            def expert_weight(turn, q, s):
                act.wait_ge(s_dots, turn * TURN + s + 1)
                nc.scalar.activation(act_out[:, s:s + 1], act_in[:, s:s + 1], ACT.Gelu).then_inc(s_gelu, 1)
                act.wait_ge(s_gelu, turn * TURN + s + 1)
                nc.scalar.mul(weight[:, s:s + 1], gate[:, bass.ds(q * TURN + s, 1)],
                              act_out[:, s:s + 1]).then_inc(s_weight, 1)
                act.wait_ge(s_weight, turn * TURN + s + 1)
                act.wait_ge(s_free, turn * TURN + s + 1)
                nc.scalar.mul(diag[:, s % RING, :], ident, weight[:, s:s + 1]).then_inc(s_diag, 1)

            def exp_logits(turn):
                act.wait_ge(s_route, OPEN + ROUTE_STEPS * turn + 10)
                nc.scalar.activation(expd, logits, ACT.Exp).then_inc(s_exp, 1)

            def expert_turn(t, q, t_next=None, q_next=None):
                turn = t * PAIRS + q
                act.wait_ge(s_route, OPEN + ROUTE_STEPS * (turn + 1))
                for s in range(TURN):
                    expert_weight(turn, q, s)
                    if t_next is not None and s == COPY_SLOT:
                        copy_score(t_next, q_next)
                    if t_next is not None and s == EXP_SLOT:
                        exp_logits(turn + 1)

            def expert_tile(t, last):
                with act.Fori(0, PAIRS - 1) as q:
                    expert_turn(t, q, t, q + 1)
                if last:
                    expert_turn(t, PAIRS - 1)
                else:
                    square2(t + 1)
                    copy_h2_t(t + 1)
                    expert_turn(t, PAIRS - 1, t + 1, 0)
                act.wait_ge(s_fin, OPEN + 4 * t + 2)
                nc.scalar.activation(squares, y, ACT.Square, accum_out=stat[:, 8:9]).then_inc(s_ssq3, 1)
                root(stat[:, 8:9], stat[:, 9:10], s_ssq3, 2 * t, 1.0 / D)

            square2(0)
            copy_h2_t(0)
            copy_score(0, 0)
            exp_logits(0)
            with act.Fori(0, TILES - 1) as t:
                expert_tile(t, False)
            expert_tile(TILES - 1, True)

        @block.vector
        def _(dve):
            dve.sem_inc(s_x1, OPEN)
            dve.sem_inc(s_route, OPEN)
            dve.sem_inc(s_fin, OPEN)
            dve.wait_ge(s_cact, 1)
            nc.vector.memset(ones, 1.0).then_inc(s_ones, 1)

            def sum_ada(stage, total, base):
                for k in range(KC):
                    if k == 0:
                        step = nc.vector.tensor_scalar(total, stage[:, k, :], c_act[:, k:k + 1], None, ALU.mult)
                    else:
                        dve.wait_ge(s_acc, base + k)
                        step = nc.vector.scalar_tensor_tensor(out=total, in0=stage[:, k, :], scalar=c_act[:, k:k + 1],
                                                              in1=total, op0=ALU.mult, op1=ALU.add)
                    step.then_inc(s_acc, 1)

            def sum_early(j):
                dve.wait_ge(s_ada_w[j % 2], 16 * (j // 2 + 1))
                if j >= 2:
                    dve.wait_ge(s_ada_ps, j - 1)
                sum_ada(ada_stage[j % 2], ada_sum[j % 2], KC * j)

            def copy_early(j):
                dve.wait_ge(s_ada_ps, j + 1)
                nc.vector.tensor_copy(mod[:, j // 2, (j % 2) * HALF:(j % 2 + 1) * HALF],
                                      ps_ada[j % 2]).then_inc(s_mod, 1)

            def sum_late(t):
                dve.wait_ge(s_ada_w[0], 16 * (EARLY // 2 + t))
                sum_ada(ada_stage[0], ada_sum[0], KC * (EARLY - 1 + t))

            def copy_late(t):
                dve.wait_ge(s_ada_ps, EARLY + t)
                nc.vector.tensor_copy(mod_rows[:, bass.ds((EARLY - 1 + t) * HALF, HALF)], ps_y).then_inc(s_mod, 1)

            def fold_gain(row, gain):
                nc.vector.scalar_tensor_tensor(out=mod[:, row, :], in0=mod[:, row, :], scalar=1.0,
                                               in1=gain, op0=ALU.add, op1=ALU.mult).then_inc(s_scales, 1)

            for j in range(4):
                sum_early(j)
                if j > 0:
                    copy_early(j - 1)
            copy_early(3)
            dve.wait_ge(s_mod, 4)
            dve.wait_ge(s_g1, 16)
            fold_gain(SCALE1, g1[:, :])

            def mask_w_spatial():
                dve.wait_ge(s_small, 96)
                w_sp_v = w_sp_t.rearrange("p (g t) -> p g t", g=GROUPS)
                nc.vector.tensor_tensor(w_sp_v, w_sp_v, tril_t.unsqueeze(1).to_broadcast([P, GROUPS, P]),
                                        ALU.mult).then_inc(s_masked, 1)

            def norm1(t):
                dve.wait_ge(s_ssq1, 2 * (t + 1))
                nc.vector.reciprocal(stat[:, 2:3], stat[:, 1:2]).then_inc(s_norm1, 1)
                dve.wait_ge(s_norm1, 2 * t + 1)
                nc.vector.scalar_tensor_tensor(out=h, in0=x_in, scalar=stat[:, 2:3], in1=mod[:, SCALE1, :],
                                               op0=ALU.mult, op1=ALU.mult).then_inc(s_norm1, 1)
                dve.wait_ge(s_norm1, 2 * t + 2)
                nc.vector.tensor_tensor(h, h, mod[:, SHIFT1, :], ALU.add).then_inc(s_h, 1)

            def layer_norm_v(t):
                dve.wait_ge(s_v, t + 1)
                nc.vector.bn_stats(v_stats[:, :], ps_v).then_inc(s_ln, 1)
                dve.wait_ge(s_ln, 6 * t + 1)
                apart(dve)
                nc.vector.bn_aggr(v_mean_var[:, :], v_stats[:, :]).then_inc(s_ln, 1)
                dve.wait_ge(s_v_root, t + 1)
                nc.vector.reciprocal(stat[:, 13:14], stat[:, 12:13]).then_inc(s_ln, 1)
                dve.wait_ge(s_ln, 6 * t + 3)
                dve.wait_ge(s_sgu, t)
                nc.vector.tensor_scalar(vn, ps_v, v_mean_var[:, 0:1], stat[:, 13:14],
                                        ALU.subtract, ALU.mult).then_inc(s_ln, 1)
                dve.wait_ge(s_ln, 6 * t + 4)
                nc.vector.tensor_tensor(vn, vn, ln_g, ALU.mult).then_inc(s_ln, 1)
                dve.wait_ge(s_ln, 6 * t + 5)
                nc.vector.tensor_tensor(vn, vn, ln_b[:, :], ALU.add).then_inc(s_ln, 1)

            def mix(t):
                dve.wait_ge(s_sgu, t + 1)
                nc.vector.tensor_tensor(gated, ps_sgu, b_sp, ALU.add).then_inc(s_gated, 1)
                dve.wait_ge(s_gated, t + 1)
                dve.wait_ge(s_u_sb, t + 1)
                dve.wait_ge(s_o, OPEN + t)
                nc.vector.tensor_tensor(mixed_t[:, GROUPS:KC, :].rearrange("p g t -> p (g t)"), gated, u_t,
                                        ALU.mult).then_inc(s_mixed, 1)
                dve.wait_ge(s_y, OPEN + t + 1)
                nc.vector.tensor_tensor(mixed_t[:, 0:GROUPS, :], ps_y.rearrange("p (g t) -> p g t", g=GROUPS),
                                        p_scale[:, :].unsqueeze(2).to_broadcast([P, GROUPS, P]),
                                        ALU.mult).then_inc(s_mixed, 1)

            def residual1(t):
                dve.wait_ge(s_o, OPEN + t + 1)
                dve.wait_ge(s_x1_free, OPEN + t)
                nc.vector.tensor_tensor(x1, ps_wide[:, :], mod[:, GATE1, :], ALU.mult).then_inc(s_x1, 1)
                dve.wait_ge(s_x1, OPEN + 2 * t + 1)
                dve.wait_ge(s_x_res, 16 * (t + 1))
                nc.vector.tensor_tensor(x1, x1, x_res, ALU.add).then_inc(s_x1, 1)

            dve.wait_ge(s_scales, 1)
            norm1(0)
            sum_early(4)
            copy_early(4)
            sum_early(5)
            copy_early(5)
            mask_w_spatial()
            norm1(1)
            layer_norm_v(0)
            dve.wait_ge(s_mod, EARLY)
            with dve.Fori(1, TILES - 1) as t:
                mix(t - 1)
                norm1(t + 1)
                residual1(t - 1)
                layer_norm_v(t)
                sum_late(t)
                copy_late(t)
            mix(TILES - 2)
            residual1(TILES - 2)
            layer_norm_v(TILES - 1)
            mix(TILES - 1)
            residual1(TILES - 1)
            nc.vector.memset(ln_b[:, 0:HALF // 2], 0.0).then_inc(s_zeroed, 1)
            dve.wait_ge(s_mod, 2 * N_MOD)
            dve.wait_ge(s_rows, 32)
            fold_gain(SCALE2, g2[:, :])

            for s in range(SIDES):
                dve.wait_ge(s_fold, s + 1)
                nc.vector.tensor_copy(key_map[:, 4:8, s * KEYS:(s + 1) * KEYS],
                                      ps_fold[s % 2][:, HALF:D].rearrange("p (k n) -> p k n", k=4)).then_inc(s_fold_v, 1)

            dve.wait_ge(s_scales, 2)

            def norm2(t):
                dve.wait_ge(s_ssq2, 2 * (t + 1))
                nc.vector.reciprocal(stat[:, 6:7], stat[:, 5:6]).then_inc(s_norm2, 1)
                dve.wait_ge(s_norm2, 2 * t + 1)
                nc.vector.scalar_tensor_tensor(out=h2_next[:, :], in0=x1_next[:, :], scalar=stat[:, 6:7],
                                               in1=mod[:, SCALE2, :], op0=ALU.mult, op1=ALU.mult).then_inc(s_norm2, 1)
                dve.wait_ge(s_norm2, 2 * t + 2)
                nc.vector.tensor_tensor(h2_next[:, :], h2_next[:, :], mod[:, SHIFT2, :], ALU.add).then_inc(s_h2, 1)

            def route_step(n, t, q):
                base = ROUTE_STEPS * (t * PAIRS + q)
                if n == 0:
                    dve.wait_ge(s_score_sb, OPEN + t * PAIRS + q + 1)
                    apart(dve)
                    for b in range(4):
                        last = nc.vector.max(top_s[:, b, 0:8], score[:, b, :])
                    last.then_inc(s_route, 1)
                    return
                dve.wait_ge(s_route, OPEN + base + n)
                if n in (1, 2, 3, 5, 6, 7, 8):
                    apart(dve)
                if n == 1:
                    for b in range(4):
                        nc.vector.max_index(top_i[:, b, 0:8], top_s[:, b, 0:8], score[:, b, :])
                        last = nc.vector.match_replace(score2[:, b, :], top_s[:, b, 0:8], score[:, b, :], LOWEST)
                elif n == 2:
                    for b in range(4):
                        last = nc.vector.max(top_s[:, b, 8:16], score2[:, b, :])
                elif n == 3:
                    for b in range(4):
                        last = nc.vector.max_index(top_i[:, b, 8:16], top_s[:, b, 8:16], score2[:, b, :])
                elif n == 4:
                    nc.vector.tensor_copy(top_f[:, :, :], top_i[:, :, :])
                    s_v4 = top_s[:, :, :].rearrange("p (h e) k -> p h e k", e=2)
                    for i in range(PAIR):
                        last = nc.vector.tensor_tensor(
                            cand[:, i, :].rearrange("p (a b) -> p a b", a=TOPK),
                            s_v4[:, i, 0, :].unsqueeze(2).to_broadcast([P, TOPK, TOPK]),
                            s_v4[:, i, 1, :].unsqueeze(1).to_broadcast([P, TOPK, TOPK]), ALU.add)
                elif n == 5:
                    for i in range(PAIR):
                        last = nc.vector.max(best[:, i, 0:8], cand[:, i, :])
                elif n == 6:
                    for i in range(PAIR):
                        nc.vector.max_index(sel[:, i, 0:8], best[:, i, 0:8], cand[:, i, :])
                        last = nc.vector.match_replace(cand2[:, i, :], best[:, i, 0:8], cand[:, i, :], LOWEST)
                elif n == 7:
                    for i in range(PAIR):
                        last = nc.vector.max(best[:, i, 8:16], cand2[:, i, :])
                elif n == 8:
                    for i in range(PAIR):
                        last = nc.vector.max_index(sel[:, i, 8:16], best[:, i, 8:16], cand2[:, i, :])
                elif n == 9:
                    nc.vector.tensor_single_scalar(sel_ab[:, 0, :, :], sel[:, :, :], 4, ALU.logical_shift_right)
                    nc.vector.tensor_single_scalar(sel_ab[:, 1, :, :], sel[:, :, :], TOPK - 1, ALU.bitwise_and)
                    last = nc.vector.tensor_tensor(
                        logits.rearrange("p (h k) -> p h k", h=PAIR),
                        best[:, :, :], best[:, :, 0:1].to_broadcast([P, PAIR, TOPK]), ALU.subtract)
                elif n == 10:
                    last = nc.vector.tensor_copy(sel_f[:, :, :, :], sel_ab[:, :, :, :])
                elif n == 11:
                    for i in range(PAIR):
                        for e, onehot in enumerate((cand, cand2)):
                            last = nc.vector.tensor_tensor(
                                onehot[:, i, :].rearrange("p (k a) -> p k a", a=TOPK),
                                sel_f[:, e, i, :].unsqueeze(2).to_broadcast([P, TOPK, TOPK]),
                                iota16.unsqueeze(1).to_broadcast([P, TOPK, TOPK]), ALU.is_equal)
                elif n == 12:
                    for i in range(PAIR):
                        for e, onehot in enumerate((cand, cand2)):
                            v = onehot[:, i, :].rearrange("p (k a) -> p k a", a=TOPK)
                            last = nc.vector.tensor_tensor(
                                v, v, top_f[:, 2 * i + e, :].unsqueeze(1).to_broadcast([P, TOPK, TOPK]), ALU.mult)
                elif n == 13:
                    for e, onehot in enumerate((cand, cand2)):
                        last = nc.vector.tensor_reduce(
                            found[:, e, :, :].rearrange("p h k -> p (h k)"),
                            onehot[:, :, :].rearrange("p h (k a) -> p (h k) a", a=TOPK), AX_X, ALU.add)
                elif n == ROWS_STEP - 1:
                    last = nc.vector.scalar_tensor_tensor(
                        out=expert_rows[:, bass.ds(q * TURN, TURN)],
                        in0=found[:, 0, :, :].rearrange("p h k -> p (h k)"), scalar=float(KEYS),
                        in1=found[:, 1, :, :].rearrange("p h k -> p (h k)"), op0=ALU.mult, op1=ALU.add)
                elif n == ROWS_STEP:
                    dve.wait_ge(s_exp, t * PAIRS + q + 1)
                    last = nc.vector.tensor_reduce(sums[:, 0, :], exp_v, AX_X, ALU.add)
                elif n == ROWS_STEP + 1:
                    last = nc.vector.reciprocal(sums[:, 1, :], sums[:, 0, :])
                else:
                    last = nc.vector.tensor_tensor(
                        gate[:, bass.ds(q * TURN, TURN)].rearrange("p (h k) -> p h k", h=PAIR), exp_v,
                        sums[:, 1, :].unsqueeze(2).to_broadcast([P, PAIR, TOPK]), ALU.mult)
                last.then_inc(s_route, 1)

            def dot(turn, s):
                dve.wait_ge(s_row[s % RING], 16 * (turn * (TURN // RING) + s // RING + 1))
                down = ring[:, s % RING, 0:D]
                nc.vector.tensor_tensor_reduce(down, down, h2_cur, 1.0, 0.0,
                                                      ALU.mult, ALU.add, act_in[:, s:s + 1]).then_inc(s_dots, 1)

            def take_h2(t):
                dve.wait_ge(s_tr2, 2 * (t + 1))
                if not isinstance(t, int) or t > 0:
                    dve.wait_ge(s_dots, t * SLOTS)
                nc.vector.tensor_copy(h2_cur, h2_next[:, :]).then_inc(s_h2c, 1)

            def finish(t):
                dve.wait_ge(s_sum, t + 1)
                dve.wait_ge(s_y_free, OPEN + t)
                nc.vector.tensor_tensor(y, ps_sum[:, :], mod[:, GATE2, :], ALU.mult).then_inc(s_fin, 1)
                dve.wait_ge(s_fin, OPEN + 4 * t + 1)
                dve.wait_ge(s_x1f, 16 * (t + 1))
                nc.vector.tensor_tensor(y, y, x1_fin, ALU.add).then_inc(s_fin, 1)
                dve.wait_ge(s_ssq3, 2 * (t + 1))
                nc.vector.reciprocal(stat[:, 10:11], stat[:, 9:10]).then_inc(s_rms, 1)
                dve.wait_ge(s_rms, t + 1)
                nc.vector.scalar_tensor_tensor(out=y, in0=y, scalar=stat[:, 10:11], in1=gf[:, :],
                                               op0=ALU.mult, op1=ALU.mult).then_inc(s_fin, 2)

            def expert_turn(t, q, t_next=None, q_next=None):
                turn = t * PAIRS + q
                dve.wait_ge(s_h2c, t + 1)
                for s in range(TURN):
                    dot(turn, s)
                    if t_next is None:
                        continue
                    if 0 <= s - ROUTE_SLOT < ROWS_STEP:
                        route_step(s - ROUTE_SLOT, t_next, q_next)
                    if s in (GATE_SLOT, GATE_SLOT + 2, GATE_SLOT + 4):
                        route_step(ROWS_STEP + (s - GATE_SLOT) // 2, t_next, q_next)

            def expert_tile(t, last):
                with dve.Fori(0, PAIRS - 1) as q:
                    expert_turn(t, q, t, q + 1)
                if last:
                    expert_turn(t, PAIRS - 1)
                else:
                    norm2(t + 1)
                    expert_turn(t, PAIRS - 1, t + 1, 0)
                    take_h2(t + 1)
                finish(t)

            norm2(0)
            for n in range(ROUTE_STEPS):
                route_step(n, 0, 0)
            take_h2(0)
            with dve.Fori(0, TILES - 1) as t:
                expert_tile(t, False)
            expert_tile(TILES - 1, True)


def kernel(x, c, w_ada, b_ada, g_norm1, w_in, w_pool, pool_scale, sgu_ln_g, sgu_ln_b, w_spatial, b_spatial,
           w_out, g_norm2, w_query, sub_keys, expert_down, expert_up, g_final):
    import concourse.bacc as bacc
    from concourse.bass_utils import run_bass_kernel_spmd

    rows = np.ascontiguousarray
    arrays = {
        "x": rows(x), "c": rows(c), "w_ada": rows(w_ada), "b_ada": rows(b_ada).reshape(-1),
        "g_norm1": rows(g_norm1).reshape(-1), "w_in": rows(w_in), "w_pool": rows(w_pool),
        "pool_scale": rows(np.asarray(pool_scale).reshape(GROUPS, P).T),
        "sgu_ln_g": rows(sgu_ln_g).reshape(-1), "sgu_ln_b": rows(sgu_ln_b).reshape(-1),
        "w_spatial_t": rows(np.transpose(np.asarray(w_spatial)[0], (2, 0, 1))).reshape(P, GROUPS * P),
        "b_spatial": rows(b_spatial).reshape(-1),
        "w_out": rows(w_out), "g_norm2": rows(g_norm2).reshape(-1),
        "w_query_t": rows(np.transpose(np.asarray(w_query)[0].reshape(D, SIDES, P), (2, 1, 0))),
        "sub_keys_t": rows(np.transpose(np.asarray(sub_keys)[0].reshape(SIDES, KEYS, P), (2, 0, 1))),
        "experts": np.concatenate([np.asarray(expert_down)[0], np.asarray(expert_up)[0]], axis=1),
        "g_final": rows(g_final).reshape(-1),
        "constants": shape_constants(),
    }
    nc = bacc.Bacc("TRN2", target_bir_lowering=False, num_devices=1)
    handles = [nc.dram_tensor(name, a.shape, F32, kind="ExternalInput").ap() for name, a in arrays.items()]
    x1_dram = nc.dram_tensor("x1_scratch", (TILES, P, D), F32).ap()
    out = nc.dram_tensor("out", (1, SEQ, D), F32, kind="ExternalOutput").ap()
    build(nc, *handles, x1_dram, out)
    result = run_bass_kernel_spmd(nc, [arrays], core_ids=[0])
    return result.results[0]["out"]
```

```python
from contextlib import ExitStack

import numpy as np
import concourse.bass as bass
from concourse import mybir

F32 = mybir.dt.float32
U32 = mybir.dt.uint32
BF16 = mybir.dt.bfloat16
ALU = mybir.AluOpType
ACT = mybir.ActivationFunctionType
AX_X = mybir.AxisListType.X

P = 128
D = 1024
SEQ = 1024
TILES = SEQ // P
KC = D // P
HALF = 512
POOL_WINDOWS = (2, 4, 8, 16)
GROUPS = len(POOL_WINDOWS)
HALO = max(POOL_WINDOWS)
IN_WIDTH = 3 * HALF
N_MOD = 6
HEADS = 8
SIDES = 2 * HEADS
KEYS = 128
TOPK = 16
SLOTS = HEADS * TOPK
EPS = 1e-6
LOWEST = -3.0e38

PAIR = 2
PAIRS = HEADS // PAIR
RING = 8
TURN = PAIR * TOPK
ROWS_STEP = 15
ROUTE_STEPS = 18
SCORE_SLOT = 6
COPY_SLOT = 7
ROUTE_SLOT = 8
EXP_SLOT = 18
GATE_SLOT = 22
ADA_STEPS = KC + 1
EARLY = 6
DIRECT = (1, 3)
SUMMED = (0, 2, 4, 5)
OPEN = 1

C_IDENT = 0
C_FIRST = P
C_TRIL = C_FIRST + GROUPS * P
C_IOTA = C_TRIL + P
C_EPS = C_IOTA + TOPK
C_ALL = C_EPS + 1


def shape_constants():
    out = np.zeros((P, C_ALL), np.float32)
    out[:, C_IDENT:C_IDENT + P] = np.eye(P)
    s, t = np.arange(P)[:, None], np.arange(P)[None, :]
    for g, w in enumerate(POOL_WINDOWS):
        out[:, C_FIRST + g * P:C_FIRST + (g + 1) * P] = 1.0 / np.minimum(t + 1.0, w)
    out[:, C_TRIL:C_TRIL + P] = s <= t
    out[:, C_IOTA:C_EPS] = np.arange(TOPK)
    out[:, C_EPS] = EPS
    return out


def build(nc, x, c, w_ada, b_ada, g_norm1, w_in, w_pool, pool_scale, sgu_ln_g, sgu_ln_b, w_spatial_t,
          b_spatial, w_out, g_norm2, w_query_t, sub_keys_t, experts, g_final, constants, x1_dram, out):
    with ExitStack() as ctx:
        def sb(name, shape, dt=F32):
            return ctx.enter_context(nc.sbuf_tensor(name, shape, dt))

        def sem(name):
            return ctx.enter_context(nc.semaphore(name))

        region_a = sb("region_a", [P, 20 * 1024])
        w_in_sb = region_a[:, 0:KC * IN_WIDTH].rearrange("p (k n) -> p k n", k=KC)
        w_out_sb = region_a[:, KC * IN_WIDTH:KC * (IN_WIDTH + D)].rearrange("p (k n) -> p k n", k=KC)
        ring = region_a[:, 0:RING * 2 * D].rearrange("p (r n) -> p r n", r=RING)
        FIRST_SLOTS = 5
        assert FIRST_SLOTS * 2 * D <= KC * IN_WIDTH
        SPARE = RING * 2 * D
        h2_cur = region_a[:, SPARE:SPARE + D]
        squares = region_a[:, SPARE + D:SPARE + 2 * D]
        x1_fin = region_a[:, SPARE + 2 * D:SPARE + 3 * D]
        y = region_a[:, SPARE + 3 * D:SPARE + 4 * D]

        region_b = sb("region_b", [P, 16 * 1024])
        key_map = region_b[:, :].rearrange("p (q k n) -> p q k n", q=PAIRS, k=KC)
        QUARTER = KC * HALF
        ada_stage = [part.rearrange("p (k n) -> p k n", k=KC) for part in (
            region_b[:, QUARTER:2 * QUARTER], region_b[:, 0:QUARTER],
            region_a[:, KC * IN_WIDTH:KC * IN_WIDTH + QUARTER],
            region_a[:, KC * IN_WIDTH + QUARTER:KC * IN_WIDTH + 2 * QUARTER])]
        at = [2 * QUARTER]

        def temp(n):
            at[0] += n
            assert at[0] <= PAIRS * QUARTER
            return region_b[:, at[0] - n:at[0]]

        x_in_and_h = temp(2 * D)
        x_in, h = x_in_and_h[:, 0:D], x_in_and_h[:, D:2 * D]
        h_t = temp(D).rearrange("p (k t) -> p k t", k=KC)
        a_t = temp(GROUPS * (HALO + P)).rearrange("p (g t) -> p g t", g=GROUPS)
        assert at[0] <= 3 * QUARTER
        at[0] = 3 * QUARTER
        x_res = temp(D)
        mixed_t = temp(D).rearrange("p (k t) -> p k t", k=KC)
        c_wide = x_res.rearrange("p (k n) -> p k n", k=KC)
        vn = temp(HALF)
        u_t = temp(HALF)
        pooled_t = temp(HALF)
        gated = temp(HALF)

        mod = sb("mod", [P, N_MOD, D])
        mod_rows = mod[:, :, :].rearrange("p m d -> p (m d)")
        SHIFT1, SCALE1, GATE1, SHIFT2, SCALE2, GATE2 = range(N_MOD)
        gf = sb("gf", [P, D])
        keys_t = [part.rearrange("p (s k) -> p s k", s=SIDES // 2) for part in (gf[:, :], y)]
        const = sb("const", [P, C_ALL])
        ident = const[:, C_IDENT:C_IDENT + P]
        first_factors = const[:, C_FIRST:C_FIRST + GROUPS * P].rearrange("p (g t) -> p g t", g=GROUPS)
        tril_t = const[:, C_TRIL:C_TRIL + P]
        iota16 = const[:, C_IOTA:C_IOTA + TOPK]
        eps = const[:, C_EPS:C_EPS + 1]
        small_w = sb("small_w", [P, 4 * HALF])
        w_pool_sb = small_w[:, 0:HALF]
        w_sp_t = small_w[:, HALF:2 * HALF]
        b_sp = small_w[:, 2 * HALF:3 * HALF]
        ln_g = small_w[:, 3 * HALF:4 * HALF]
        ln_b = sb("ln_b", [P, HALF])
        p_scale = sb("p_scale", [P, GROUPS])
        c_cols = sb("c_cols", [P, KC])
        c_act = sb("c_act", [P, KC])

        x1_next = sb("x1_next", [P, D])
        h2_next = sb("h2_next", [P, D])
        h2_t = sb("h2_t", [P, KC, P])
        ones = h2_t[:, 0, :]
        ada_sum = [h2_t[:, 1:5, :].rearrange("p k t -> p (k t)"),
                   mixed_t[:, 0:4, :].rearrange("p k t -> p (k t)")]
        g1, g2 = x1_next, h2_next
        diag = sb("diag", [P, RING, P])
        x1 = diag[:, :, :].rearrange("p r t -> p (r t)")

        window_sums = sb("window_sums", [P, (2 * GROUPS - 1) * (HALO + P)])
        sums_2_8, sums_4_16 = (part.rearrange("p (g t) -> p g t", t=HALO + P) for part in (
            window_sums[:, 0:GROUPS * (HALO + P)], window_sums[:, GROUPS * (HALO + P):]))

        class Routing:

            def __init__(self, wide, tops, chosen, best, logits, expd):
                by_side, by_head = (dict(b=4), dict(h=PAIR))
                self.score = wide[:, 0:HALF].rearrange("p (b k) -> p b k", **by_side)
                self.cand = wide[:, HALF:2 * HALF].rearrange("p (h k) -> p h k", **by_head)
                self.cand2 = wide[:, 2 * HALF:3 * HALF].rearrange("p (h k) -> p h k", **by_head)
                self.score2 = wide[:, 2 * HALF:3 * HALF].rearrange("p (b k) -> p b k", **by_side)
                self.top_s, self.top_f = (tops[:, i * 4 * TOPK:(i + 1) * 4 * TOPK].rearrange("p (b k) -> p b k", b=4)
                                          for i in range(2))
                self.sel_f, self.found = (chosen[:, i * 2 * TURN:(i + 1) * 2 * TURN].rearrange(
                    "p (e h k) -> p e h k", e=2, h=PAIR) for i in range(2))
                self.best = best[:, 0:TURN].rearrange("p (h k) -> p h k", h=PAIR)
                self.logits, self.expd = logits, expd

        usual = Routing(small_w, window_sums[:, 0:P], window_sums[:, P:2 * P], window_sums[:, 2 * P:2 * P + TURN],
                        *(small_w[:, 3 * HALF + i * SLOTS:3 * HALF + i * SLOTS + TURN] for i in range(2)))
        early = x_in_and_h[:, 3 * HALF:4 * HALF]
        first = Routing(x_in_and_h, early[:, 0:P], early[:, P:2 * P], early[:, 2 * P:2 * P + TURN],
                        early[:, 3 * P:3 * P + TURN], early[:, 3 * P + TURN:3 * P + 2 * TURN])
        gate = small_w[:, 3 * HALF + 2 * SLOTS:3 * HALF + 3 * SLOTS]
        act_in, act_out, weight = (small_w[:, 3 * HALF + 3 * SLOTS + i * TURN:3 * HALF + 3 * SLOTS + (i + 1) * TURN]
                                   for i in range(3))
        top_i = sb("top_i", [P, 4, TOPK], U32)
        sel = sb("sel", [P, PAIR, TOPK], U32)
        sel_ab = sb("sel_ab", [P, 2, PAIR, TOPK], U32)
        expert_rows = sb("expert_rows", [P, SLOTS], U32)
        row_stage = [sb(f"row_stage{i}", [P, TOPK], U32) for i in range(PAIR)]
        stat = sb("stat", [P, 16])
        v_stats = sb("v_stats", [P, 6])
        v_mean_var = sb("v_mean_var", [P, 2])
        sums = sb("sums", [P, 2, PAIR])
        zero_bf = ln_b[:, 0:HALF // 2].bitcast(BF16)

        banks = [ctx.enter_context(nc.psum_tensor(f"banks{i}", [P, D], F32)) for i in range(4)]
        ps_wide = banks[0]
        ps_v, ps_a = banks[1][:, 0:HALF], banks[1][:, HALF:D]
        ps_u = banks[2][:, 0:HALF]
        ps_y, ps_sgu = banks[3][:, 0:HALF], banks[3][:, HALF:D]
        ps_ada = [banks[3][:, 0:HALF], banks[3][:, HALF:D]]
        ps_fold_0 = [ps_wide[:, 0:HALF], ps_wide[:, HALF:D]]
        ps_fold = [ps_v, ps_a, ps_y, ps_sgu]
        ps_h2 = banks[1]
        ps_score = banks[2][:, 0:HALF]
        ps_sum = banks[0]

        s_c = sem("c_loaded")
        s_const = sem("const_loaded")
        s_b_ada = sem("b_ada_loaded")
        s_g1 = sem("g_norm1_loaded")
        s_g2 = sem("g_norm2_loaded")
        s_gf = sem("g_final_loaded")
        s_ln_rows = sem("ln_rows_loaded")
        s_small = sem("small_weights_loaded")
        s_ada_w = [sem(f"ada_stage{i}_loaded") for i in range(4)]
        s_w_in = [sem(f"w_in_{n}_loaded") for n in "vau"]
        s_w_out = sem("w_out_loaded")
        s_x_in = sem("x_in_loaded")
        s_x_res = sem("x_res_loaded")
        s_cact = sem("c_act_ready")
        s_ones = sem("ones_and_c_wide_ready")
        s_acc = sem("ada_sum_steps")
        s_ada_ps = sem("ada_psum_ready")
        s_mod = sem("mod_rows_ready")
        s_scales = sem("scales_folded")
        s_masked = sem("w_spatial_masked")
        s_init = sem("start_values_set")
        s_ssq1 = sem("ssq1_ready")
        s_norm1 = sem("norm1_steps")
        s_h = sem("h_ready")
        s_tr = sem("h_transposed")
        s_ht = sem("h_t_ready")
        s_v = sem("v_psum_ready")
        s_a = sem("a_psum_ready")
        s_u = sem("u_psum_ready")
        s_ln = sem("ln_steps")
        s_v_root = sem("v_root_ready")
        s_a_sb = sem("a_ready")
        s_u_sb = sem("u_t_ready")
        s_windows = sem("window_sum_steps")
        s_halo = sem("halo_moved")
        s_pooled = sem("pooled_ready")
        s_y = sem("y_psum_ready")
        s_sgu = sem("sgu_psum_ready")
        s_gated = sem("gated_ready")
        s_mixed = sem("mixed_ready")
        s_o = sem("out_psum_ready")
        s_x1 = sem("x1_steps")
        s_x1_st = sem("x1_stored")
        s_x1_free = sem("x1_free")
        s_wq = [sem(f"w_query{q}_loaded") for q in range(PAIRS)]
        s_keys = [sem("keys01_loaded"), sem("keys23_loaded")]
        s_fold = sem("fold_psum_ready")
        s_map = sem("key_map_halves_ready")
        s_x1n = sem("x1_next_loaded")
        s_ssq2 = sem("ssq2_ready")
        s_norm2 = sem("norm2_steps")
        s_h2 = sem("h2_ready")
        s_tr2 = sem("h2_transposed")
        s_h2t = sem("h2_t_ready")
        s_score = sem("score_psum_ready")
        s_score_sb = sem("score_ready")
        s_route = sem("route_steps")
        s_staged = sem("rows_staged")
        s_exp = sem("exp_ready")
        s_h2c = sem("h2_cur_ready")
        s_row = [sem(f"expert_row{r}_landed") for r in range(RING)]
        s_free = sem("ring_slots_free")
        s_dots = sem("dots_ready")
        s_gelu = sem("gelu_ready")
        s_weight = sem("weights_ready")
        s_diag = sem("diags_ready")
        s_zeroed = sem("sums_zeroed")
        s_sum = sem("sums_ready")
        s_fin = sem("final_steps")
        s_ssq3 = sem("ssq3_ready")
        s_rms = sem("final_norm_steps")
        s_x1f = sem("x1_final_copied")
        s_out = sem("out_stored")
        s_y_free = sem("y_free")

        x_v = x.rearrange("b (t p) d -> (b t) p d", p=P)
        out_v = out.rearrange("b (t p) d -> (b t) p d", p=P)
        ada_v = w_ada.rearrange("l (p k) n -> (l p) k n", k=KC)
        w_in_v = w_in.rearrange("l (k p) n -> p (l k) n", p=P)
        w_out_v = w_out.rearrange("l (k p) n -> p (l k) n", p=P)

        block = ctx.enter_context(nc.Block())

        def apart(engine):
            engine.nop(nofuse=True)

        def mod_before(t):
            return 2 * N_MOD if isinstance(t, int) and t > TILES - 2 else EARLY + t

        @block.sync
        def _(sp):
            sp.sem_inc(s_x1_free, OPEN)
            sp.sem_inc(s_y_free, OPEN)
            sp.dma_start(c_cols[:, :], c.rearrange("b (p k) -> (b p) k", k=KC)).then_inc(s_c, 16)

            def load_ada(j):
                sp.dma_start(ada_stage[j % 4], ada_v[:, :, j * HALF:(j + 1) * HALF]).then_inc(s_ada_w[j % 4], 16)

            def load_x_in(t):
                sp.wait_ge(s_norm1, 2 * t)
                sp.dma_start(x_in, x_v[t]).then_inc(s_x_in, 16)

            def load_ada_late(t):
                sp.wait_ge(s_acc, ADA_STEPS * (len(SUMMED) - 1 + t))
                sp.dma_start(ada_stage[0], ada_v[:, :, bass.ds((EARLY - 1 + t) * HALF, HALF)]).then_inc(s_ada_w[0], 16)

            load_ada(0)
            sp.dma_start(mod[0:1, :, :].rearrange("p m d -> p (m d)"), b_ada.unsqueeze(0)).then_inc(s_b_ada, 16)
            load_ada(1)
            load_ada(2)
            load_ada(3)
            sp.dma_start(const[:, :], constants).then_inc(s_const, 16)
            sp.dma_start(x_in, x_v[0]).then_inc(s_x_in, 16)
            sp.dma_start(g1[:, :], g_norm1.partition_broadcast(P)).then_inc(s_g1, 16)
            for n, col in enumerate((2 * HALF, 0, HALF)):
                sp.dma_start(w_in_sb[:, :, col:col + HALF], w_in_v[:, :, col:col + HALF]).then_inc(s_w_in[n], 16)
            sp.dma_start(ln_g, sgu_ln_g.partition_broadcast(P)).then_inc(s_ln_rows, 16)
            sp.dma_start(ln_b[:, :], sgu_ln_b.partition_broadcast(P)).then_inc(s_ln_rows, 16)
            load_x_in(1)
            sp.wait_ge(s_acc, ADA_STEPS)
            load_ada(4)
            sp.wait_ge(s_ada_ps, 2)
            load_ada(5)
            sp.dma_start(w_sp_t, w_spatial_t).then_inc(s_small, 16)
            sp.dma_start(w_pool_sb.rearrange("p (g d) -> p g d", g=GROUPS),
                         w_pool.rearrange("l g c d -> c (l g) d")).then_inc(s_small, 16)
            sp.dma_start(b_sp, b_spatial.partition_broadcast(P)).then_inc(s_small, 16)
            sp.dma_start(p_scale[:, :], pool_scale).then_inc(s_small, 16)
            sp.wait_ge(s_ada_ps, 4)
            sp.dma_start(w_out_sb, w_out_v).then_inc(s_w_out, 16)

            def load_x_res(t):
                if not isinstance(t, int) or t >= 1:
                    sp.wait_ge(s_x1, OPEN + 2 * t)
                sp.dma_start(x_res, x_v[t]).then_inc(s_x_res, 16)

            def mixer_loads(t):
                load_x_in(t)
                load_x_res(t - 1)

            def store_x1(t):
                sp.wait_ge(s_x1, OPEN + 2 * (t + 1))
                sp.dma_start(x1_dram[t], x1).then_inc(s_x1_st, 16)
                sp.wait_ge(s_x1_st, 16 * (t + 1))
                sp.sem_inc(s_x1_free, 1)

            load_x_res(0)
            load_ada_late(1)
            sp.dma_start(g2[:, :], g_norm2.partition_broadcast(P)).then_inc(s_g2, 16)
            sp.dma_start(keys_t[0], sub_keys_t[:, 0:SIDES // 2, :]).then_inc(s_keys[0], 16)

            def load_w_query(q):
                sp.dma_start(key_map[:, q, :, :], w_query_t[:, q, :, :]).then_inc(s_wq[q], 16)

            sp.wait_ge(s_acc, ADA_STEPS * len(SUMMED))
            load_w_query(0)
            with sp.Fori(2, TILES - 1) as t:
                mixer_loads(t)
                load_ada_late(t)
                store_x1(t - 2)
            mixer_loads(TILES - 1)
            sp.wait_ge(s_scales, 1)
            sp.dma_start(x1_next[:, :], x1_dram[0]).then_inc(s_x1n, 16)
            sp.wait_ge(s_acc, ADA_STEPS * (2 * N_MOD - len(DIRECT)))
            load_w_query(1)
            store_x1(TILES - 3)
            load_x_res(TILES - 1)
            store_x1(TILES - 2)
            sp.wait_ge(s_u, TILES)
            sp.sem_inc(s_free, FIRST_SLOTS)
            sp.wait_ge(s_pooled, TILES)
            sp.wait_ge(s_route, OPEN + ROUTE_STEPS)
            load_w_query(2)
            sp.wait_ge(s_o, OPEN + TILES)
            sp.dma_start(keys_t[1], sub_keys_t[:, SIDES // 2:SIDES, :]).then_inc(s_keys[1], 16)
            sp.wait_ge(s_x1, OPEN + 2 * TILES)
            load_w_query(3)
            sp.sem_inc(s_free, RING - FIRST_SLOTS)
            store_x1(TILES - 1)
            sp.wait_ge(s_fold, 2 * SIDES)
            sp.dma_start(gf[:, :], g_final.partition_broadcast(P)).then_inc(s_gf, 16)

            def expert_loads(t, last):
                if not last:
                    sp.wait_ge(s_x1f, t + 1)
                    sp.dma_start(x1_next[:, :], x1_dram[t + 1]).then_inc(s_x1n, 16)
                sp.wait_ge(s_fin, OPEN + 4 * (t + 1))
                sp.dma_start(out_v[t], y).then_inc(s_out, 16)
                sp.wait_ge(s_out, 16 * (t + 1))
                sp.sem_inc(s_y_free, 1)

            with sp.Fori(0, TILES - 1) as t:
                expert_loads(t, False)
            expert_loads(TILES - 1, True)

        @block.gpsimd
        def _(pool):
            nc.gpsimd.memset(a_t[:, :, 0:HALO], 0.0).then_inc(s_init, 1)

            def gather_turn(t, q):
                turn = t * PAIRS + q
                for i in range(PAIR):
                    pool.wait_ge(s_route, OPEN + ROUTE_STEPS * turn + ROWS_STEP)
                    pool.wait_ge(s_free, turn * TURN + i * TOPK + 1)
                    apart(pool)
                    nc.gpsimd.tensor_copy(row_stage[i][:, :],
                                          expert_rows[:, bass.ds((q * PAIR + i) * TOPK, TOPK)]).then_inc(s_staged, 1)
                    pool.wait_ge(s_staged, turn * PAIR + i + 1)
                    for k in range(TOPK):
                        s = i * TOPK + k
                        pool.wait_ge(s_free, turn * TURN + s + 1)
                        apart(pool)
                        nc.gpsimd.indirect_dma_start(
                            ring[:, s % RING, :], None, experts,
                            bass.IndirectOffsetOnAxis(ap=row_stage[i][:, k:k + 1], axis=0),
                        ).then_inc(s_row[s % RING], 16)

            with pool.Fori(0, TILES) as t:
                with pool.Fori(0, PAIRS) as q:
                    gather_turn(t, q)

        @block.tensor
        def _(pe):
            pe.sem_inc(s_y, OPEN)
            pe.sem_inc(s_o, OPEN)

            def spread_ada(total, bank):
                nc.tensor.matmul(bank, ones, total, start=True, stop=True).then_inc(s_ada_ps, 1)

            def spread_early(j, copied):
                pe.wait_ge(s_acc, ADA_STEPS * (SUMMED.index(j) + 1))
                if copied:
                    pe.wait_ge(s_mod, copied)
                spread_ada(ada_sum[SUMMED.index(j) % 2], ps_ada[j % 2])

            def direct(j, copied):
                pe.wait_ge(s_ada_w[j], 16)
                if copied:
                    pe.wait_ge(s_mod, copied)
                for k in range(KC):
                    nc.tensor.matmul(ps_ada[j % 2], c_wide[:, k, :], ada_stage[j][:, k, :], start=(k == 0), stop=False)
                nc.tensor.matmul(ps_ada[j % 2], ones[0:1, :], mod_rows[0:1, j * HALF:(j + 1) * HALF],
                                 start=False, stop=True).then_inc(s_ada_ps, 1)

            def spread_late(t):
                pe.wait_ge(s_acc, ADA_STEPS * (len(SUMMED) + t))
                pe.wait_ge(s_mixed, 2 * t)
                spread_ada(ada_sum[0], ps_y)

            pe.wait_ge(s_ones, 2)
            pe.wait_ge(s_b_ada, 16)
            spread_early(0, 0)
            direct(1, 0)
            direct(3, 2)
            spread_early(2, 1)
            pe.wait_ge(s_const, 16)

            def transposes(t):
                pe.wait_ge(s_h, t + 1)
                for k in range(KC):
                    last = nc.tensor.transpose(ps_wide[:, k * P:(k + 1) * P], h[:, k * P:(k + 1) * P], ident)
                    if k % 4 == 3:
                        last.then_inc(s_tr, 1)

            def projection(t):
                pe.wait_ge(s_ht, 2 * (t + 1))
                if isinstance(t, int) and t == 0:
                    pe.wait_ge(s_w_in[0], 16)
                for k in range(KC):
                    last = nc.tensor.matmul(ps_v, h_t[:, k, :], w_in_sb[:, k, 2 * HALF:3 * HALF],
                                            start=(k == 0), stop=(k == KC - 1))
                last.then_inc(s_v, 1)
                if isinstance(t, int) and t == 0:
                    pe.wait_ge(s_w_in[1], 16)
                if not isinstance(t, int) or t > 0:
                    pe.wait_ge(s_a_sb, t)
                for g in range(GROUPS):
                    for k in range(KC):
                        last = nc.tensor.matmul(ps_a[:, g * P:(g + 1) * P],
                                                w_in_sb[:, k, g * P:(g + 1) * P], h_t[:, k, :],
                                                start=(k == 0), stop=(k == KC - 1))
                last.then_inc(s_a, 1)
                if isinstance(t, int) and t == 0:
                    pe.wait_ge(s_w_in[2], 16)
                for g in range(GROUPS):
                    for k in range(KC):
                        last = nc.tensor.matmul(ps_u[:, g * P:(g + 1) * P],
                                                w_in_sb[:, k, HALF + g * P:HALF + (g + 1) * P], h_t[:, k, :],
                                                start=(k == 0), stop=(k == KC - 1))
                last.then_inc(s_u, 1)

            def mix_spatial(t):
                if isinstance(t, int) and t == 0:
                    pe.wait_ge(s_mod, EARLY)
                pe.wait_ge(s_ln, 6 * (t + 1))
                for g in range(GROUPS):
                    cols = slice(g * P, (g + 1) * P)
                    last = nc.tensor.matmul(ps_sgu[:, cols], vn[:, cols], w_sp_t[:, cols], start=True, stop=True)
                last.then_inc(s_sgu, 1)

            def mix_pooled(t):
                pe.wait_ge(s_pooled, t + 1)
                pe.wait_ge(s_mod, mod_before(t))
                for g in range(GROUPS):
                    cols = slice(g * P, (g + 1) * P)
                    last = nc.tensor.matmul(ps_y[:, cols], w_pool_sb[:, cols], pooled_t[:, cols], start=True, stop=True)
                last.then_inc(s_y, 1)

            def mix_out(t):
                for part in (0, 1):
                    pe.wait_ge(s_mixed, 2 * t + 1 + part)
                    for n in range(2):
                        for i in range(GROUPS):
                            k = (1 - part) * GROUPS + i
                            last = nc.tensor.matmul(ps_wide[:, n * HALF:(n + 1) * HALF], mixed_t[:, k, :],
                                                    w_out_sb[:, k, n * HALF:(n + 1) * HALF],
                                                    start=(part == 0 and i == 0), stop=(part == 1 and i == GROUPS - 1))
                last.then_inc(s_o, 1)

            def mix(t):
                mix_spatial(t)
                mix_pooled(t)
                pe.wait_ge(s_ht, 2 * (t + 2))
                mix_out(t)

            transposes(0)
            projection(0)
            spread_early(4, 4)
            transposes(1)
            spread_early(5, 4)
            pe.wait_ge(s_masked, 1)
            mix_spatial(0)
            pe.wait_ge(s_small, 64)
            mix_pooled(0)
            pe.wait_ge(s_w_out, 16)
            pe.wait_ge(s_ht, 4)
            mix_out(0)
            projection(1)
            spread_late(1)

            def mixer_iteration(t):
                pe.wait_ge(s_x1, OPEN + 2 * (t - 1))
                transposes(t)
                mix(t - 1)
                projection(t)

            with pe.Fori(2, TILES - 1) as t:
                mixer_iteration(t)
                spread_late(t)

            def fold_pair(q):
                pe.wait_ge(s_keys[q // 2], 16)
                pe.wait_ge(s_wq[q], 16)
                for half in range(8 * q, 8 * (q + 1)):
                    s, k0 = half // 2, half % 2 * (KC // 2)
                    room = ps_fold_0[half % 2] if q == 0 else ps_fold[half % 4]
                    held = 2 if q == 0 else 4
                    if half % 8 >= held or q >= 2:
                        pe.wait_ge(s_map, half - held + 1)
                    for k in range(k0, k0 + KC // 2):
                        last = nc.tensor.matmul(room[:, (k - k0) * KEYS:(k - k0 + 1) * KEYS],
                                                key_map[:, q, k, s % 4 * KEYS:(s % 4 + 1) * KEYS],
                                                keys_t[q // 2][:, s % (SIDES // 2), :], start=True, stop=True)
                    last.then_inc(s_fold, 1)

            def transposes2(t):
                pe.wait_ge(s_h2, t + 1)
                for k in range(KC):
                    last = nc.tensor.transpose(ps_h2[:, k * P:(k + 1) * P], h2_next[:, k * P:(k + 1) * P], ident)
                    if k % 4 == 3:
                        last.then_inc(s_tr2, 1)

            def scores(t, q):
                pe.wait_ge(s_h2t, 2 * (t + 1))
                pe.wait_ge(s_score_sb, OPEN + t * PAIRS + q)
                for k in range(KC):
                    columns = key_map[:, bass.ds(q, 1), k, :].rearrange("p o n -> p (o n)")
                    last = nc.tensor.matmul(ps_score, h2_t[:, k, :], columns,
                                            start=(k == 0), stop=(k == KC - 1))
                last.then_inc(s_score, 1)

            def clear_sums(stop):
                for n in range(2):
                    last = nc.tensor.matmul(ps_sum[:, n * HALF:(n + 1) * HALF], zero_bf[:, 0:P], zero_bf,
                                            start=not stop, stop=stop, skip_group_check=True)
                return last

            def add_expert(turn, s):
                pe.wait_ge(s_diag, turn * TURN + s + 1)
                for n in range(2):
                    last = nc.tensor.matmul(ps_sum[:, n * HALF:(n + 1) * HALF], diag[:, s % RING, :],
                                            ring[:, s % RING, D + n * HALF:D + (n + 1) * HALF],
                                            start=False, stop=False, skip_group_check=True)
                last.then_inc(s_free, 1)

            def expert_turn(t, q, t_next=None, q_next=None):
                for s in range(TURN):
                    add_expert(t * PAIRS + q, s)
                    if t_next is not None and s == SCORE_SLOT:
                        scores(t_next, q_next)

            def expert_tile(t, last):
                pe.wait_ge(s_fin, OPEN + 4 * t)
                clear_sums(False)
                with pe.Fori(0, PAIRS - 1) as q:
                    expert_turn(t, q, t, q + 1)
                if last:
                    expert_turn(t, PAIRS - 1)
                else:
                    transposes2(t + 1)
                    expert_turn(t, PAIRS - 1, t + 1, 0)
                clear_sums(True).then_inc(s_sum, 1)

            pe.wait_ge(s_x1, OPEN + 2 * (TILES - 2))
            transposes(TILES - 1)
            mix_spatial(TILES - 2)
            mix_pooled(TILES - 2)
            pe.wait_ge(s_ht, 2 * TILES)
            fold_pair(0)
            pe.wait_ge(s_a_sb, TILES - 1)
            transposes2(0)
            pe.wait_ge(s_u_sb, TILES - 1)
            pe.wait_ge(s_map, 8)
            scores(0, 0)
            mix_out(TILES - 2)
            pe.wait_ge(s_h2t, 2)
            pe.wait_ge(s_score_sb, OPEN + 1)
            projection(TILES - 1)
            mix_spatial(TILES - 1)
            mix_pooled(TILES - 1)
            pe.wait_ge(s_x1, OPEN + 2 * (TILES - 1))
            mix_out(TILES - 1)
            for q in range(1, PAIRS):
                fold_pair(q)
            pe.wait_ge(s_map, 2 * SIDES)
            pe.wait_ge(s_zeroed, 1)
            pe.wait_ge(s_x1, OPEN + 2 * TILES)
            with pe.Fori(0, TILES - 1) as t:
                expert_tile(t, False)
            expert_tile(TILES - 1, True)

        @block.scalar
        def _(act):
            act.sem_inc(s_score_sb, OPEN)
            act.wait_ge(s_c, 16)
            nc.scalar.activation(c_act[:, :], c_cols[:, :], ACT.Silu).then_inc(s_cact, 1)

            def root(mean_sq, out_col, steps, base, scale):
                act.wait_ge(steps, base + 1)
                nc.scalar.activation(out_col, mean_sq, ACT.Sqrt, bias=eps, scale=scale).then_inc(steps, 1)

            def square1(t):
                act.wait_ge(s_x_in, 16 * (t + 1))
                act.wait_ge(s_tr, 2 * t)
                nc.scalar.activation(h, x_in, ACT.Square, accum_out=stat[:, 0:1]).then_inc(s_ssq1, 1)
                root(stat[:, 0:1], stat[:, 1:2], s_ssq1, 2 * t, 1.0 / D)

            def copy_h_t(t):
                for n in range(2):
                    act.wait_ge(s_tr, 2 * t + n + 1)
                    act.wait_ge(s_u, t)
                    nc.scalar.copy(h_t[:, 4 * n:4 * n + 4, :].rearrange("p k t -> p (k t)"),
                                   ps_wide[:, n * HALF:(n + 1) * HALF]).then_inc(s_ht, 1)

            def copy_a_u(t):
                act.wait_ge(s_ln, 6 * t + 2)
                nc.scalar.activation(stat[:, 12:13], v_mean_var[:, 1:2], ACT.Sqrt, bias=eps).then_inc(s_v_root, 1)
                act.wait_ge(s_a, t + 1)
                act.wait_ge(s_halo, t)
                nc.scalar.copy(a_t[:, :, HALO:HALO + P],
                               ps_a.rearrange("p (g t) -> p g t", g=GROUPS)).then_inc(s_a_sb, 1)
                act.wait_ge(s_u, t + 1)
                act.wait_ge(s_mixed, 2 * t)
                nc.scalar.copy(u_t, ps_u).then_inc(s_u_sb, 1)

            def copy_early(j, spread):
                act.wait_ge(s_ada_ps, spread)
                nc.scalar.copy(mod_rows[:, j * HALF:(j + 1) * HALF], ps_ada[j % 2]).then_inc(s_mod, 1)

            copy_early(0, 1)
            copy_early(1, 2)
            act.wait_ge(s_const, 16)
            square1(0)
            copy_early(3, 3)
            copy_early(2, 4)
            copy_h_t(0)
            square1(1)
            copy_a_u(0)
            copy_early(4, 5)
            copy_early(5, 6)
            with act.Fori(1, TILES - 1) as t:
                copy_h_t(t)
                square1(t + 1)
                copy_a_u(t)
            def square2(t):
                act.wait_ge(s_x1n, 16 * (t + 1))
                if not isinstance(t, int) or t > 0:
                    act.wait_ge(s_h2c, t)
                nc.scalar.activation(h2_next[:, :], x1_next[:, :], ACT.Square,
                                     accum_out=stat[:, 4:5]).then_inc(s_ssq2, 1)
                root(stat[:, 4:5], stat[:, 5:6], s_ssq2, 2 * t, 1.0 / D)

            def copy_fold(q):
                for half in range(8 * q, 8 * (q + 1)):
                    s, k0 = half // 2, half % 2 * (KC // 2)
                    room = ps_fold_0[half % 2] if q == 0 else ps_fold[half % 4]
                    act.wait_ge(s_fold, half + 1)
                    nc.scalar.copy(key_map[:, q, k0:k0 + KC // 2, s % 4 * KEYS:(s % 4 + 1) * KEYS],
                                   room.rearrange("p (k n) -> p k n", k=KC // 2)).then_inc(s_map, 1)

            def copy_h2_t(t):
                for n in range(2):
                    act.wait_ge(s_tr2, 2 * t + n + 1)
                    nc.scalar.copy(h2_t[:, 4 * n:4 * n + 4, :].rearrange("p k t -> p (k t)"),
                                   ps_h2[:, n * HALF:(n + 1) * HALF]).then_inc(s_h2t, 1)

            def copy_score(t, q, use=usual):
                turn = t * PAIRS + q
                act.wait_ge(s_score, turn + 1)
                act.wait_ge(s_route, OPEN + ROUTE_STEPS * turn)
                nc.scalar.copy(use.score[:, :, :].rearrange("p b k -> p (b k)"), ps_score).then_inc(s_score_sb, 1)

            def expert_weight(turn, q, s):
                act.wait_ge(s_dots, turn * TURN + s + 1)
                nc.scalar.activation(act_out[:, s:s + 1], act_in[:, s:s + 1], ACT.Gelu).then_inc(s_gelu, 1)
                act.wait_ge(s_gelu, turn * TURN + s + 1)
                nc.scalar.mul(weight[:, s:s + 1], gate[:, bass.ds(q * TURN + s, 1)],
                              act_out[:, s:s + 1]).then_inc(s_weight, 1)
                act.wait_ge(s_weight, turn * TURN + s + 1)
                act.wait_ge(s_free, turn * TURN + s + 1)
                nc.scalar.mul(diag[:, s % RING, :], ident, weight[:, s:s + 1]).then_inc(s_diag, 1)

            def exp_logits(turn, use=usual):
                act.wait_ge(s_route, OPEN + ROUTE_STEPS * turn + 10)
                nc.scalar.activation(use.expd, use.logits, ACT.Exp).then_inc(s_exp, 1)

            def expert_turn(t, q, t_next=None, q_next=None):
                turn = t * PAIRS + q
                act.wait_ge(s_route, OPEN + ROUTE_STEPS * (turn + 1))
                for s in range(TURN):
                    expert_weight(turn, q, s)
                    if t_next is not None and s == COPY_SLOT:
                        copy_score(t_next, q_next)
                    if t_next is not None and s == EXP_SLOT:
                        exp_logits(turn + 1)

            def expert_tile(t, last):
                with act.Fori(0, PAIRS - 1) as q:
                    expert_turn(t, q, t, q + 1)
                if last:
                    expert_turn(t, PAIRS - 1)
                else:
                    square2(t + 1)
                    copy_h2_t(t + 1)
                    expert_turn(t, PAIRS - 1, t + 1, 0)
                act.wait_ge(s_fin, OPEN + 4 * t + 2)
                nc.scalar.activation(squares, y, ACT.Square, accum_out=stat[:, 8:9]).then_inc(s_ssq3, 1)
                root(stat[:, 8:9], stat[:, 9:10], s_ssq3, 2 * t, 1.0 / D)

            copy_h_t(TILES - 1)
            act.wait_ge(s_scales, 2)
            square2(0)
            copy_fold(0)
            act.wait_ge(s_ada_ps, 2 * N_MOD)
            copy_h2_t(0)
            act.wait_ge(s_norm1, 2 * TILES)
            act.wait_ge(s_tr, 2 * TILES)
            copy_score(0, 0, first)
            copy_a_u(TILES - 1)
            exp_logits(0, first)
            for q in range(1, PAIRS):
                copy_fold(q)
            act.wait_ge(s_x1_free, OPEN + TILES)
            with act.Fori(0, TILES - 1) as t:
                expert_tile(t, False)
            expert_tile(TILES - 1, True)

        @block.vector
        def _(dve):
            dve.sem_inc(s_x1, OPEN)
            dve.sem_inc(s_route, OPEN)
            dve.sem_inc(s_fin, OPEN)
            dve.wait_ge(s_cact, 1)
            nc.vector.memset(ones, 1.0).then_inc(s_ones, 1)
            nc.vector.tensor_copy(c_wide, c_act[:, :].unsqueeze(2).to_broadcast([P, KC, P])).then_inc(s_ones, 1)

            def sum_ada(stage, total, row, base):
                for k in range(KC):
                    if k == 0:
                        step = nc.vector.tensor_scalar(total, stage[:, k, :], c_act[:, k:k + 1], None, ALU.mult)
                    else:
                        dve.wait_ge(s_acc, base + k)
                        step = nc.vector.scalar_tensor_tensor(out=total, in0=stage[:, k, :], scalar=c_act[:, k:k + 1],
                                                              in1=total, op0=ALU.mult, op1=ALU.add)
                    step.then_inc(s_acc, 1)
                dve.wait_ge(s_acc, base + KC)
                dve.wait_ge(s_b_ada, 16)
                nc.vector.tensor_tensor(total[0:1, :], total[0:1, :], row, ALU.add).then_inc(s_acc, 1)

            def sum_early(j):
                n = SUMMED.index(j)
                dve.wait_ge(s_ada_w[j % 4], 16 * (j // 4 + 1))
                if n >= 2:
                    dve.wait_ge(s_ada_ps, (1, 4)[n - 2])
                sum_ada(ada_stage[j % 4], ada_sum[n % 2], mod_rows[0:1, j * HALF:(j + 1) * HALF], ADA_STEPS * n)

            def sum_late(t):
                dve.wait_ge(s_ada_w[0], 16 * (2 + t))
                sum_ada(ada_stage[0], ada_sum[0], mod_rows[0:1, bass.ds((EARLY - 1 + t) * HALF, HALF)],
                        ADA_STEPS * (len(SUMMED) - 1 + t))

            def copy_late(t):
                dve.wait_ge(s_ada_ps, EARLY + t)
                apart(dve)
                nc.vector.tensor_copy(mod_rows[:, bass.ds((EARLY - 1 + t) * HALF, HALF)], ps_y).then_inc(s_mod, 1)

            def fold_gain(row, gain):
                nc.vector.scalar_tensor_tensor(out=mod[:, row, :], in0=mod[:, row, :], scalar=1.0,
                                               in1=gain, op0=ALU.add, op1=ALU.mult).then_inc(s_scales, 1)

            sum_early(0)
            sum_early(2)
            dve.wait_ge(s_mod, 4)
            dve.wait_ge(s_g1, 16)
            fold_gain(SCALE1, g1[:, :])

            def mask_w_spatial():
                dve.wait_ge(s_small, 64)
                w_sp_v = w_sp_t.rearrange("p (g t) -> p g t", g=GROUPS)
                nc.vector.tensor_tensor(w_sp_v, w_sp_v, tril_t.unsqueeze(1).to_broadcast([P, GROUPS, P]),
                                        ALU.mult).then_inc(s_masked, 1)

            def norm1(t):
                dve.wait_ge(s_ssq1, 2 * (t + 1))
                nc.vector.reciprocal(stat[:, 2:3], stat[:, 1:2]).then_inc(s_norm1, 1)
                dve.wait_ge(s_norm1, 2 * t + 1)
                nc.vector.scalar_tensor_tensor(out=h, in0=x_in, scalar=stat[:, 2:3], in1=mod[:, SCALE1, :],
                                               op0=ALU.mult, op1=ALU.mult).then_inc(s_norm1, 1)
                dve.wait_ge(s_norm1, 2 * t + 2)
                nc.vector.tensor_tensor(h, h, mod[:, SHIFT1, :], ALU.add).then_inc(s_h, 1)

            def layer_norm_v(t):
                dve.wait_ge(s_v, t + 1)
                nc.vector.bn_stats(v_stats[:, :], ps_v).then_inc(s_ln, 1)
                dve.wait_ge(s_ln, 6 * t + 1)
                apart(dve)
                nc.vector.bn_aggr(v_mean_var[:, :], v_stats[:, :]).then_inc(s_ln, 1)
                dve.wait_ge(s_v_root, t + 1)
                nc.vector.reciprocal(stat[:, 13:14], stat[:, 12:13]).then_inc(s_ln, 1)
                dve.wait_ge(s_ln, 6 * t + 3)
                dve.wait_ge(s_sgu, t)
                nc.vector.tensor_scalar(vn, ps_v, v_mean_var[:, 0:1], stat[:, 13:14],
                                        ALU.subtract, ALU.mult).then_inc(s_ln, 1)
                dve.wait_ge(s_ln, 6 * t + 4)
                nc.vector.tensor_tensor(vn, vn, ln_g, ALU.mult).then_inc(s_ln, 1)
                dve.wait_ge(s_ln, 6 * t + 5)
                nc.vector.tensor_tensor(vn, vn, ln_b[:, :], ALU.add).then_inc(s_ln, 1)

            def pool_windows(t):
                first_tile = isinstance(t, int) and t == 0
                base = 4 * t if first_tile else 4 * t + 1
                end = HALO + P
                dve.wait_ge(s_a_sb, t + 1)
                if first_tile:
                    dve.wait_ge(s_init, 1)
                else:
                    dve.wait_ge(s_halo, t)
                nc.vector.tensor_tensor(sums_2_8[:, :, 1:end], a_t[:, :, 1:end], a_t[:, :, 0:end - 1],
                                        ALU.add).then_inc(s_windows, 1)
                dve.wait_ge(s_windows, base + 1)
                nc.vector.tensor_tensor(sums_4_16[:, :, 3:end], sums_2_8[:, 1:GROUPS, 3:end],
                                        sums_2_8[:, 1:GROUPS, 1:end - 2], ALU.add).then_inc(s_windows, 1)
                dve.wait_ge(s_windows, base + 2)
                nc.vector.tensor_tensor(sums_2_8[:, 2:GROUPS, 7:end], sums_4_16[:, 1:GROUPS - 1, 7:end],
                                        sums_4_16[:, 1:GROUPS - 1, 3:end - 4], ALU.add).then_inc(s_windows, 1)
                dve.wait_ge(s_windows, base + 3)
                nc.vector.tensor_tensor(sums_4_16[:, 2:3, 15:end], sums_2_8[:, 3:4, 15:end],
                                        sums_2_8[:, 3:4, 7:end - 8], ALU.add).then_inc(s_windows, 1)
                dve.wait_ge(s_windows, base + 4)
                dve.wait_ge(s_y, OPEN + t)
                pooled = pooled_t.rearrange("p (g t) -> p g t", g=GROUPS)
                whole = [sums_2_8[:, 0, HALO:end], sums_4_16[:, 0, HALO:end],
                         sums_2_8[:, 2, HALO:end], sums_4_16[:, 2, HALO:end]]
                for g, w in enumerate(POOL_WINDOWS):
                    if first_tile:
                        last = nc.vector.tensor_tensor(pooled[:, g, :], whole[g], first_factors[:, g, :], ALU.mult)
                    else:
                        last = nc.vector.scalar_tensor_tensor(out=pooled[:, g, :], in0=whole[g], scalar=1.0 / w,
                                                              in1=a_t[:, g, HALO:end],
                                                              op0=ALU.mult, op1=ALU.subtract)
                if first_tile:
                    last.then_inc(s_windows, 1)
                    dve.wait_ge(s_windows, 5)
                    last = nc.vector.tensor_tensor(pooled, pooled, a_t[:, :, HALO:end], ALU.subtract)
                last.then_inc(s_pooled, 1)
                if not isinstance(t, int) or t < TILES - 1:
                    nc.vector.tensor_copy(a_t[:, :, 0:HALO], a_t[:, :, P:end]).then_inc(s_halo, 1)

            def mix(t):
                dve.wait_ge(s_sgu, t + 1)
                nc.vector.tensor_tensor(gated, ps_sgu, b_sp, ALU.add).then_inc(s_gated, 1)
                dve.wait_ge(s_gated, t + 1)
                dve.wait_ge(s_u_sb, t + 1)
                dve.wait_ge(s_o, OPEN + t)
                nc.vector.tensor_tensor(mixed_t[:, GROUPS:KC, :].rearrange("p g t -> p (g t)"), gated, u_t,
                                        ALU.mult).then_inc(s_mixed, 1)
                dve.wait_ge(s_y, OPEN + t + 1)
                nc.vector.tensor_tensor(mixed_t[:, 0:GROUPS, :], ps_y.rearrange("p (g t) -> p g t", g=GROUPS),
                                        p_scale[:, :].unsqueeze(2).to_broadcast([P, GROUPS, P]),
                                        ALU.mult).then_inc(s_mixed, 1)

            def residual1(t):
                dve.wait_ge(s_o, OPEN + t + 1)
                dve.wait_ge(s_x1_free, OPEN + t)
                nc.vector.tensor_tensor(x1, ps_wide[:, :], mod[:, GATE1, :], ALU.mult).then_inc(s_x1, 1)
                dve.wait_ge(s_x1, OPEN + 2 * t + 1)
                dve.wait_ge(s_x_res, 16 * (t + 1))
                nc.vector.tensor_tensor(x1, x1, x_res, ALU.add).then_inc(s_x1, 1)

            dve.wait_ge(s_scales, 1)
            norm1(0)
            norm1(1)
            dve.wait_ge(s_ln_rows, 32)
            layer_norm_v(0)
            sum_early(4)
            dve.wait_ge(s_const, 16)
            mask_w_spatial()
            sum_early(5)
            pool_windows(0)
            dve.wait_ge(s_mod, EARLY)
            with dve.Fori(1, TILES - 1) as t:
                mix(t - 1)
                norm1(t + 1)
                residual1(t - 1)
                sum_late(t)
                layer_norm_v(t)
                pool_windows(t)
                copy_late(t)
            def norm2(t):
                dve.wait_ge(s_ssq2, 2 * (t + 1))
                nc.vector.reciprocal(stat[:, 6:7], stat[:, 5:6]).then_inc(s_norm2, 1)
                dve.wait_ge(s_norm2, 2 * t + 1)
                nc.vector.scalar_tensor_tensor(out=h2_next[:, :], in0=x1_next[:, :], scalar=stat[:, 6:7],
                                               in1=mod[:, SCALE2, :], op0=ALU.mult, op1=ALU.mult).then_inc(s_norm2, 1)
                dve.wait_ge(s_norm2, 2 * t + 2)
                nc.vector.tensor_tensor(h2_next[:, :], h2_next[:, :], mod[:, SHIFT2, :], ALU.add).then_inc(s_h2, 1)

            def route_step(n, t, q, use=usual):
                exp_v = use.expd.rearrange("p (h k) -> p h k", h=PAIR)
                base = ROUTE_STEPS * (t * PAIRS + q)
                if n == 0:
                    dve.wait_ge(s_score_sb, OPEN + t * PAIRS + q + 1)
                    apart(dve)
                    for b in range(4):
                        last = nc.vector.max(use.top_s[:, b, 0:8], use.score[:, b, :])
                    last.then_inc(s_route, 1)
                    return
                dve.wait_ge(s_route, OPEN + base + n)
                if n in (1, 2, 3, 5, 6, 7, 8):
                    apart(dve)
                if n == 1:
                    for b in range(4):
                        nc.vector.max_index(top_i[:, b, 0:8], use.top_s[:, b, 0:8], use.score[:, b, :])
                        last = nc.vector.match_replace(use.score2[:, b, :], use.top_s[:, b, 0:8],
                                                       use.score[:, b, :], LOWEST)
                elif n == 2:
                    for b in range(4):
                        last = nc.vector.max(use.top_s[:, b, 8:16], use.score2[:, b, :])
                elif n == 3:
                    for b in range(4):
                        last = nc.vector.max_index(top_i[:, b, 8:16], use.top_s[:, b, 8:16], use.score2[:, b, :])
                elif n == 4:
                    nc.vector.tensor_copy(use.top_f[:, :, :], top_i[:, :, :])
                    s_v4 = use.top_s[:, :, :].rearrange("p (h e) k -> p h e k", e=2)
                    for i in range(PAIR):
                        last = nc.vector.tensor_tensor(
                            use.cand[:, i, :].rearrange("p (a b) -> p a b", a=TOPK),
                            s_v4[:, i, 0, :].unsqueeze(2).to_broadcast([P, TOPK, TOPK]),
                            s_v4[:, i, 1, :].unsqueeze(1).to_broadcast([P, TOPK, TOPK]), ALU.add)
                elif n == 5:
                    for i in range(PAIR):
                        last = nc.vector.max(use.best[:, i, 0:8], use.cand[:, i, :])
                elif n == 6:
                    for i in range(PAIR):
                        nc.vector.max_index(sel[:, i, 0:8], use.best[:, i, 0:8], use.cand[:, i, :])
                        last = nc.vector.match_replace(use.cand2[:, i, :], use.best[:, i, 0:8],
                                                       use.cand[:, i, :], LOWEST)
                elif n == 7:
                    for i in range(PAIR):
                        last = nc.vector.max(use.best[:, i, 8:16], use.cand2[:, i, :])
                elif n == 8:
                    for i in range(PAIR):
                        last = nc.vector.max_index(sel[:, i, 8:16], use.best[:, i, 8:16], use.cand2[:, i, :])
                elif n == 9:
                    nc.vector.tensor_single_scalar(sel_ab[:, 0, :, :], sel[:, :, :], 4, ALU.logical_shift_right)
                    nc.vector.tensor_single_scalar(sel_ab[:, 1, :, :], sel[:, :, :], TOPK - 1, ALU.bitwise_and)
                    last = nc.vector.tensor_tensor(
                        use.logits.rearrange("p (h k) -> p h k", h=PAIR),
                        use.best[:, :, :], use.best[:, :, 0:1].to_broadcast([P, PAIR, TOPK]), ALU.subtract)
                elif n == 10:
                    last = nc.vector.tensor_copy(use.sel_f[:, :, :, :], sel_ab[:, :, :, :])
                elif n == 11:
                    for i in range(PAIR):
                        for e, onehot in enumerate((use.cand, use.cand2)):
                            last = nc.vector.tensor_tensor(
                                onehot[:, i, :].rearrange("p (k a) -> p k a", a=TOPK),
                                use.sel_f[:, e, i, :].unsqueeze(2).to_broadcast([P, TOPK, TOPK]),
                                iota16.unsqueeze(1).to_broadcast([P, TOPK, TOPK]), ALU.is_equal)
                elif n == 12:
                    for i in range(PAIR):
                        for e, onehot in enumerate((use.cand, use.cand2)):
                            v = onehot[:, i, :].rearrange("p (k a) -> p k a", a=TOPK)
                            last = nc.vector.tensor_tensor(
                                v, v, use.top_f[:, 2 * i + e, :].unsqueeze(1).to_broadcast([P, TOPK, TOPK]), ALU.mult)
                elif n == 13:
                    for e, onehot in enumerate((use.cand, use.cand2)):
                        last = nc.vector.tensor_reduce(
                            use.found[:, e, :, :].rearrange("p h k -> p (h k)"),
                            onehot[:, :, :].rearrange("p h (k a) -> p (h k) a", a=TOPK), AX_X, ALU.add)
                elif n == ROWS_STEP - 1:
                    last = nc.vector.scalar_tensor_tensor(
                        out=expert_rows[:, bass.ds(q * TURN, TURN)],
                        in0=use.found[:, 0, :, :].rearrange("p h k -> p (h k)"), scalar=float(KEYS),
                        in1=use.found[:, 1, :, :].rearrange("p h k -> p (h k)"), op0=ALU.mult, op1=ALU.add)
                elif n == ROWS_STEP:
                    dve.wait_ge(s_exp, t * PAIRS + q + 1)
                    last = nc.vector.tensor_reduce(sums[:, 0, :], exp_v, AX_X, ALU.add)
                elif n == ROWS_STEP + 1:
                    last = nc.vector.reciprocal(sums[:, 1, :], sums[:, 0, :])
                else:
                    last = nc.vector.tensor_tensor(
                        gate[:, bass.ds(q * TURN, TURN)].rearrange("p (h k) -> p h k", h=PAIR), exp_v,
                        sums[:, 1, :].unsqueeze(2).to_broadcast([P, PAIR, TOPK]), ALU.mult)
                last.then_inc(s_route, 1)

            def dot(turn, s):
                dve.wait_ge(s_row[s % RING], 16 * (turn * (TURN // RING) + s // RING + 1))
                down = ring[:, s % RING, 0:D]
                nc.vector.tensor_tensor_reduce(down, down, h2_cur, 1.0, 0.0,
                                               ALU.mult, ALU.add, act_in[:, s:s + 1]).then_inc(s_dots, 1)

            def take_h2(t):
                dve.wait_ge(s_tr2, 2 * (t + 1))
                if not isinstance(t, int) or t > 0:
                    dve.wait_ge(s_dots, t * SLOTS)
                nc.vector.tensor_copy(h2_cur, h2_next[:, :]).then_inc(s_h2c, 1)

            def take_x1(t):
                if not isinstance(t, int) or t > 0:
                    dve.wait_ge(s_fin, OPEN + 4 * t)
                nc.vector.tensor_copy(x1_fin, x1_next[:, :]).then_inc(s_x1f, 1)

            def finish(t):
                dve.wait_ge(s_sum, t + 1)
                dve.wait_ge(s_y_free, OPEN + t)
                nc.vector.tensor_tensor(y, ps_sum[:, :], mod[:, GATE2, :], ALU.mult).then_inc(s_fin, 1)
                dve.wait_ge(s_fin, OPEN + 4 * t + 1)
                dve.wait_ge(s_x1f, t + 1)
                nc.vector.tensor_tensor(y, y, x1_fin, ALU.add).then_inc(s_fin, 1)
                dve.wait_ge(s_ssq3, 2 * (t + 1))
                nc.vector.reciprocal(stat[:, 10:11], stat[:, 9:10]).then_inc(s_rms, 1)
                dve.wait_ge(s_rms, t + 1)
                dve.wait_ge(s_gf, 16)
                nc.vector.scalar_tensor_tensor(out=y, in0=y, scalar=stat[:, 10:11], in1=gf[:, :],
                                               op0=ALU.mult, op1=ALU.mult).then_inc(s_fin, 2)

            def expert_turn(t, q, t_next=None, q_next=None):
                turn = t * PAIRS + q
                dve.wait_ge(s_h2c, t + 1)
                for s in range(TURN):
                    dot(turn, s)
                    if t_next is None:
                        continue
                    if 0 <= s - ROUTE_SLOT < ROWS_STEP:
                        route_step(s - ROUTE_SLOT, t_next, q_next)
                    if s in (GATE_SLOT, GATE_SLOT + 2, GATE_SLOT + 4):
                        route_step(ROWS_STEP + (s - GATE_SLOT) // 2, t_next, q_next)

            def expert_tile(t, last):
                with dve.Fori(0, PAIRS - 1) as q:
                    expert_turn(t, q, t, q + 1)
                if last:
                    expert_turn(t, PAIRS - 1)
                else:
                    norm2(t + 1)
                    expert_turn(t, PAIRS - 1, t + 1, 0)
                    take_h2(t + 1)
                finish(t)
                if not last:
                    take_x1(t + 1)

            dve.wait_ge(s_mod, 2 * N_MOD)
            dve.wait_ge(s_g2, 16)
            fold_gain(SCALE2, g2[:, :])
            mix(TILES - 2)
            dve.wait_ge(s_scales, 2)
            norm2(0)
            for n in range(ROWS_STEP):
                route_step(n, 0, 0, first)
            residual1(TILES - 2)
            layer_norm_v(TILES - 1)
            pool_windows(TILES - 1)
            dve.wait_ge(s_ln, 6 * TILES)
            for n in range(ROWS_STEP, ROUTE_STEPS):
                route_step(n, 0, 0, first)
            nc.vector.memset(ln_b[:, 0:HALF // 2], 0.0).then_inc(s_zeroed, 1)
            mix(TILES - 1)
            residual1(TILES - 1)
            take_h2(0)
            take_x1(0)
            with dve.Fori(0, TILES - 1) as t:
                expert_tile(t, False)
            expert_tile(TILES - 1, True)


def kernel(x, c, w_ada, b_ada, g_norm1, w_in, w_pool, pool_scale, sgu_ln_g, sgu_ln_b, w_spatial, b_spatial,
           w_out, g_norm2, w_query, sub_keys, expert_down, expert_up, g_final):
    import concourse.bacc as bacc
    from concourse.bass_utils import run_bass_kernel_spmd

    rows = np.ascontiguousarray
    arrays = {
        "x": rows(x), "c": rows(c), "w_ada": rows(w_ada), "b_ada": rows(b_ada).reshape(-1),
        "g_norm1": rows(g_norm1).reshape(-1), "w_in": rows(w_in), "w_pool": rows(w_pool),
        "pool_scale": rows(np.asarray(pool_scale).reshape(GROUPS, P).T),
        "sgu_ln_g": rows(sgu_ln_g).reshape(-1), "sgu_ln_b": rows(sgu_ln_b).reshape(-1),
        "w_spatial_t": rows(np.transpose(np.asarray(w_spatial)[0], (2, 0, 1))).reshape(P, GROUPS * P),
        "b_spatial": rows(b_spatial).reshape(-1),
        "w_out": rows(w_out), "g_norm2": rows(g_norm2).reshape(-1),
        "w_query_t": rows(np.transpose(np.asarray(w_query)[0].reshape(KC, P, PAIRS, 4, P),
                                       (4, 2, 0, 3, 1))).reshape(P, PAIRS, KC, 4 * P),
        "sub_keys_t": rows(np.transpose(np.asarray(sub_keys)[0].reshape(SIDES, KEYS, P), (2, 0, 1))),
        "experts": np.concatenate([np.asarray(expert_down)[0], np.asarray(expert_up)[0]], axis=1),
        "g_final": rows(g_final).reshape(-1),
        "constants": shape_constants(),
    }
    nc = bacc.Bacc("TRN2", target_bir_lowering=False, num_devices=1)
    handles = [nc.dram_tensor(name, a.shape, F32, kind="ExternalInput").ap() for name, a in arrays.items()]
    x1_dram = nc.dram_tensor("x1_scratch", (TILES, P, D), F32).ap()
    out = nc.dram_tensor("out", (1, SEQ, D), F32, kind="ExternalOutput").ap()
    build(nc, *handles, x1_dram, out)
    result = run_bass_kernel_spmd(nc, [arrays], core_ids=[0])
    return result.results[0]["out"]
```
